# Optimizing a Trainium2 kernel written in Bass

```python
import math
import jax, jax.numpy as jnp
from jax import lax
import numpy as np

D_MODEL = 1024
BATCH = 1
SEQ = 256
DEPTH = 2
DEC_BATCH = 8
DEC_SEQ = 4
PAST_LEN = 2048
PAGE_SIZE = 128

N_MIXERS = 2
N_SSM_LAYERS = (DEPTH + 1) // 2
N_NSA_LAYERS = DEPTH // 2
MIX_WIDTH = D_MODEL
N_MEM = 256
MEM_HEADS = 4
MEM_HEAD_DIM = 64
MEM_WIDTH = MEM_HEADS * MEM_HEAD_DIM
SSM_WIDTH = MIX_WIDTH - MEM_WIDTH
SSM_GROUP = 16
SSM_GROUPS = SSM_WIDTH // SSM_GROUP
SSM_STATE = 64
DT_MIN = 1e-3
DT_MAX = 1e-1
NSA_HEAD_DIM = 64
NSA_HEADS = (MIX_WIDTH - MEM_WIDTH) // NSA_HEAD_DIM
NSA_KV_HEADS = 3
NSA_GROUP = NSA_HEADS // NSA_KV_HEADS
NSA_WIDTH = NSA_HEADS * NSA_HEAD_DIM
NSA_KV_WIDTH = NSA_KV_HEADS * 2 * NSA_HEAD_DIM
CMP_BLOCK = 32
CMP_STRIDE = 16
CMP_HIDDEN = 2 * NSA_HEAD_DIM
SEL_BLOCK = 64
SEL_TOP = 16
WINDOW = 512
SLC_Q_BLOCK = 32
WIN_Q_BLOCK = 128
SSM_IN = SSM_WIDTH + MEM_WIDTH
NSA_IN = NSA_WIDTH + 3 * NSA_KV_WIDTH + 3 * NSA_HEADS + MEM_WIDTH
D_FF = -(-8 * D_MODEL // (3 * 256)) * 256
RMS_EPS = 1e-6
NEG = -1e30
BIG = 1e30
SCALE = NSA_HEAD_DIM ** -0.5

kernel_name = 'hybrid_s5_nsa_memory_decoder_step'

F32 = jnp.float32

def rmsnorm(x, g):
    xf = x.astype(F32)
    y = xf * lax.rsqrt(jnp.mean(xf * xf, axis=-1, keepdims=True) + RMS_EPS)
    return (y * g.astype(F32)).astype(x.dtype)

def masked_softmax(s, mask):
    s = jnp.where(mask, s, NEG)
    p = jnp.exp(s - jnp.max(s, axis=-1, keepdims=True)) * mask
    return p / jnp.maximum(jnp.sum(p, axis=-1, keepdims=True), 1e-30)

def alibi_slopes():
    h = jnp.arange(NSA_HEADS, dtype=F32) + 1.0
    return jnp.exp2(-8.0 * h / NSA_HEADS).reshape(NSA_KV_HEADS, NSA_GROUP)

def swiglu_ffn(x, w_in, w_out):
    g, u = jnp.split(x @ w_in, 2, axis=-1)
    return (jax.nn.silu(g) * u) @ w_out

def mem_kv_proj(mem, w):
    return (mem @ w).reshape(mem.shape[0], mem.shape[1], MEM_HEADS, 2, MEM_HEAD_DIM)

def mem_attention(q, mem_kv):
    s = jnp.einsum('bthd,bnhd->bthn', q, mem_kv[..., 0, :]).astype(F32) * MEM_HEAD_DIM ** -0.5
    p = jax.nn.softmax(s, axis=-1)
    o = jnp.einsum('bthn,bnhd->bthd', p.astype(mem_kv.dtype), mem_kv[..., 1, :])
    return o.reshape(q.shape[0], q.shape[1], MEM_WIDTH)

def _linear_combine(e1, e2):
    a1, b1 = e1
    a2, b2 = e2
    return a1 * a2, a2 * b1 + b2

def s5_ssm(u, h0, a_re, a_im, log_dt, b_re, b_im, c_re, c_im, d, w_glu, b_glu):
    B, L, _ = u.shape
    lam = lax.complex(a_re.astype(F32), a_im.astype(F32))
    dt = jnp.exp(log_dt.astype(F32))[:, None]
    abar = jnp.exp(lam * dt)
    bbar = ((abar - 1.0) / lam)[..., None] * lax.complex(b_re.astype(F32), b_im.astype(F32))
    ug = u.astype(F32).reshape(B, L, SSM_GROUPS, SSM_GROUP)
    bu = lax.complex(jnp.einsum('blgj,gpj->blgp', ug, jnp.real(bbar)),
                     jnp.einsum('blgj,gpj->blgp', ug, jnp.imag(bbar)))
    bu = bu.at[:, 0].add(abar * h0)
    a = jnp.broadcast_to(abar, (1, L) + abar.shape)
    _, h = lax.associative_scan(_linear_combine, (a, bu), axis=1)
    y = (jnp.einsum('blgp,gjp->blgj', jnp.real(h), c_re.astype(F32))
         - jnp.einsum('blgp,gjp->blgj', jnp.imag(h), c_im.astype(F32)))
    y = y.reshape(B, L, SSM_WIDTH) + d.astype(F32) * u.astype(F32)
    y = jax.nn.gelu(y)
    y = y * jax.nn.sigmoid(y @ w_glu.astype(F32) + b_glu.astype(F32))
    return y.astype(u.dtype), h[:, -1]

def s5_mixer(h, h0, mem_kv, w_in, a_re, a_im, log_dt, b_re, b_im, c_re, c_im, d, w_glu, b_glu):
    B, T = h.shape[:2]
    z = h @ w_in
    y, h_last = s5_ssm(z[..., :SSM_WIDTH], h0, a_re, a_im, log_dt, b_re, b_im, c_re, c_im, d, w_glu, b_glu)
    om = mem_attention(z[..., SSM_WIDTH:].reshape(B, T, MEM_HEADS, MEM_HEAD_DIM), mem_kv)
    return jnp.concatenate([y, om.astype(y.dtype)], axis=-1), h_last

def nsa_split(z):
    B, T = z.shape[:2]
    q = z[..., :NSA_WIDTH].reshape(B, T, NSA_KV_HEADS, NSA_GROUP, NSA_HEAD_DIM)
    o = NSA_WIDTH
    kvs = []
    for _ in range(3):
        kvs.append(z[..., o:o + NSA_KV_WIDTH].reshape(B, T, NSA_KV_HEADS, 2, NSA_HEAD_DIM))
        o += NSA_KV_WIDTH
    gates = jax.nn.sigmoid(z[..., o:o + 3 * NSA_HEADS].astype(F32)).reshape(B, T, 3, NSA_KV_HEADS, NSA_GROUP)
    o += 3 * NSA_HEADS
    qm = z[..., o:].reshape(B, T, MEM_HEADS, MEM_HEAD_DIM)
    return q, kvs[0], kvs[1], kvs[2], gates, qm

def cmp_subblock_proj(kv, w1):
    B, T = kv.shape[:2]
    sub = kv.reshape(B, T // CMP_STRIDE, CMP_STRIDE, NSA_KV_HEADS, 2, NSA_HEAD_DIM)
    w = w1.reshape(CMP_BLOCK // CMP_STRIDE, CMP_STRIDE, 2, NSA_HEAD_DIM, CMP_HIDDEN)
    return jnp.einsum('bnjhce,ajcef->bnhacf', sub, w)

def cmp_tokens(proj, pe, w1, b1, w2):
    bias = jnp.einsum('jce,jcef->cf', pe, w1) + b1
    hid = proj[:, :-1, :, 0] + proj[:, 1:, :, 1] + bias
    return jnp.einsum('bnhcf,cfe->bnhce', jax.nn.gelu(hid), w2)

def cmp_attend(q, q_pos, ckv, slopes):
    n = ckv.shape[1]
    e_pos = (jnp.arange(n) + CMP_BLOCK // CMP_STRIDE) * CMP_STRIDE - 1
    dist = q_pos[:, None] - e_pos[None, :]
    s = (jnp.einsum('bqhgd,bnhd->bqhgn', q, ckv[..., 0, :]).astype(F32) * SCALE
         - slopes[None, :, :, None] * dist.astype(F32)[:, None, None, :])
    p = masked_softmax(s, (dist >= 0)[:, None, None, :])
    o = jnp.einsum('bqhgn,bnhd->bqhgd', p.astype(ckv.dtype), ckv[..., 1, :])
    return o, p

def select_blocks(p, q_pos, total_len):
    n_cmp = p.shape[-1]
    n_sel = -(-total_len // SEL_BLOCK)
    ci = jnp.arange(n_cmp)[:, None] * CMP_STRIDE
    sj = jnp.arange(n_sel)[None, :] * SEL_BLOCK
    cover = ((ci < sj + SEL_BLOCK) & (ci + CMP_BLOCK > sj)).astype(F32)
    imp = jnp.einsum('bqhgn,nj->bqhj', p, cover)
    jj = jnp.arange(n_sel)[None, :]
    cur = (q_pos // SEL_BLOCK)[:, None]
    forced = (jj == 0) | (jj == cur) | (jj == cur - 1)
    valid = jj * SEL_BLOCK <= q_pos[:, None]
    imp = jnp.where(forced[None, :, None, :], BIG, jnp.where(valid[None, :, None, :], imp, NEG))
    _, idx = lax.top_k(imp, min(SEL_TOP, n_sel))
    return idx

def block_tokens(idx):
    B, Tq, H, k = idx.shape
    return (idx[..., None] * SEL_BLOCK + jnp.arange(SEL_BLOCK)).reshape(B, Tq, H, k * SEL_BLOCK)

def slc_attend(q, q_pos, tok, kv_sel, slopes):
    dist = q_pos[None, :, None, None] - tok
    s = (jnp.einsum('bqhgd,bqhnd->bqhgn', q, kv_sel[..., 0, :]).astype(F32) * SCALE
         - slopes[None, None, :, :, None] * dist.astype(F32)[:, :, :, None, :])
    p = masked_softmax(s, (dist >= 0)[:, :, :, None, :])
    return jnp.einsum('bqhgn,bqhnd->bqhgd', p.astype(kv_sel.dtype), kv_sel[..., 1, :])

def win_attend(q, q_pos, kv, k_pos, slopes):
    dist = q_pos[:, None] - k_pos[None, :]
    mask = (dist >= 0) & (dist < WINDOW) & (k_pos[None, :] >= 0)
    s = (jnp.einsum('bqhgd,bkhd->bqhgk', q, kv[..., 0, :]).astype(F32) * SCALE
         - slopes[None, :, :, None] * dist.astype(F32)[:, None, None, :])
    p = masked_softmax(s, mask[:, None, None, :])
    return jnp.einsum('bqhgk,bkhd->bqhgd', p.astype(kv.dtype), kv[..., 1, :])

def gate_merge(gates, o_cmp, o_slc, o_win, dtype):
    o = (gates[:, :, 0, :, :, None] * o_cmp + gates[:, :, 1, :, :, None] * o_slc
         + gates[:, :, 2, :, :, None] * o_win)
    return o.reshape(o.shape[0], o.shape[1], NSA_WIDTH).astype(dtype)

def nsa_prompt(h, mem_kv, w_in, pe, w1, b1, w2, slopes):
    B, T = h.shape[:2]
    q, kv_cmp, kv_slc, kv_win, gates, qm = nsa_split(h @ w_in)
    q_pos = jnp.arange(T)
    ckv = cmp_tokens(cmp_subblock_proj(kv_cmp, w1), pe, w1, b1, w2)
    o_cmp, p = cmp_attend(q, q_pos, ckv, slopes)
    idx = select_blocks(p, q_pos, T)
    k_sel = idx.shape[-1]
    bi = jnp.arange(B)[:, None, None, None]
    hi = jnp.arange(NSA_KV_HEADS)[None, None, :, None]

    def slc_block(args):
        qb, ib, pb = args
        tok = block_tokens(ib)
        kv_sel = kv_slc[bi, jnp.minimum(tok, T - 1), hi]
        return slc_attend(qb, pb, tok, kv_sel, slopes)

    nb = T // SLC_Q_BLOCK
    o_slc = lax.map(slc_block, (
        jnp.moveaxis(q.reshape(B, nb, SLC_Q_BLOCK, NSA_KV_HEADS, NSA_GROUP, NSA_HEAD_DIM), 1, 0),
        jnp.moveaxis(idx.reshape(B, nb, SLC_Q_BLOCK, NSA_KV_HEADS, k_sel), 1, 0),
        q_pos.reshape(nb, SLC_Q_BLOCK)))
    o_slc = jnp.moveaxis(o_slc, 0, 1).reshape(q.shape)

    kv_pad = jnp.pad(kv_win, ((0, 0), (WINDOW, 0), (0, 0), (0, 0), (0, 0)))

    def win_block(n):
        start = n * WIN_Q_BLOCK
        qb = lax.dynamic_slice_in_dim(q, start, WIN_Q_BLOCK, axis=1)
        kb = lax.dynamic_slice_in_dim(kv_pad, start, WIN_Q_BLOCK + WINDOW, axis=1)
        qp = start + jnp.arange(WIN_Q_BLOCK)
        kp = start - WINDOW + jnp.arange(WIN_Q_BLOCK + WINDOW)
        return win_attend(qb, qp, kb, kp, slopes)

    o_win = jnp.moveaxis(lax.map(win_block, jnp.arange(T // WIN_Q_BLOCK)), 0, 1).reshape(q.shape)
    o = gate_merge(gates, o_cmp, o_slc, o_win, h.dtype)
    om = mem_attention(qm, mem_kv)
    new_win = kv_win[:, T - min(WINDOW, T):]
    return jnp.concatenate([o, om.astype(o.dtype)], axis=-1), (kv_cmp, kv_slc, new_win)

def nsa_sample(h, mem_kv, pool_cmp, pool_slc, win_buf, page_table, w_in, pe, w1, b1, w2, slopes):
    B, T = h.shape[:2]
    past_len = page_table.shape[1] * PAGE_SIZE
    total = past_len + T
    q, kv_cmp, kv_slc, kv_win, gates, qm = nsa_split(h @ w_in)
    q_pos = past_len + jnp.arange(T)
    past_cmp = pool_cmp[page_table].reshape(B, past_len, NSA_KV_HEADS, 2, NSA_HEAD_DIM)
    proj = cmp_subblock_proj(past_cmp, w1)
    n_new_rows = (T // CMP_STRIDE) * CMP_STRIDE
    if n_new_rows > 0:
        proj = jnp.concatenate([proj, cmp_subblock_proj(kv_cmp[:, :n_new_rows], w1)], axis=1)
    ckv = cmp_tokens(proj, pe, w1, b1, w2)
    o_cmp, p = cmp_attend(q, q_pos, ckv, slopes)
    tok = block_tokens(select_blocks(p, q_pos, total))
    bi = jnp.arange(B)[:, None, None, None]
    hi = jnp.arange(NSA_KV_HEADS)[None, None, :, None]
    tok_past = jnp.minimum(tok, past_len - 1)
    pages = page_table[bi, tok_past // PAGE_SIZE]
    kv_past = pool_slc[pages, tok_past % PAGE_SIZE, hi]
    kv_new = kv_slc[bi, jnp.clip(tok - past_len, 0, T - 1), hi]
    kv_sel = jnp.where((tok >= past_len)[..., None, None], kv_new, kv_past)
    o_slc = slc_attend(q, q_pos, tok, kv_sel, slopes)
    kv_w = jnp.concatenate([win_buf, kv_win], axis=1)
    k_pos = past_len - win_buf.shape[1] + jnp.arange(kv_w.shape[1])
    o_win = win_attend(q, q_pos, kv_w, k_pos, slopes)
    o = gate_merge(gates, o_cmp, o_slc, o_win, h.dtype)
    om = mem_attention(qm, mem_kv)
    new_win = kv_w[:, kv_w.shape[1] - min(WINDOW, total):]
    return jnp.concatenate([o, om.astype(o.dtype)], axis=-1), (kv_cmp, kv_slc, new_win)

def setup_inputs(seed: int = 0) -> dict:
    key = jax.random.key(seed)
    keys = iter(jax.random.split(key, 48))

    def nrm(shape, scale):
        return scale * jax.random.normal(next(keys), shape, jnp.float32)

    n_pages = PAST_LEN // PAGE_SIZE
    n_pool = (DEC_BATCH * n_pages * 5) // 4
    win_len = min(WINDOW, PAST_LEN)
    kv_row = (NSA_KV_HEADS, 2, NSA_HEAD_DIM)
    page_table = jax.random.permutation(next(keys), n_pool)[:DEC_BATCH * n_pages].reshape(DEC_BATCH, n_pages).astype(jnp.int32)
    ssm_a_im = jnp.pi * jnp.arange(SSM_STATE, dtype=jnp.float32) + nrm((N_SSM_LAYERS, SSM_GROUPS, SSM_STATE), 0.01)
    ssm_log_dt = jax.random.uniform(next(keys), (N_SSM_LAYERS, SSM_GROUPS), jnp.float32, math.log(DT_MIN), math.log(DT_MAX))
    x_prompt = nrm((BATCH, SEQ, D_MODEL), 1.0)
    x_sample = nrm((DEC_BATCH, DEC_SEQ, D_MODEL), 1.0)
    mem_prompt = nrm((BATCH, N_MEM, D_MODEL), 1.0)
    state_ssm_re = nrm((N_SSM_LAYERS, DEC_BATCH, SSM_GROUPS, SSM_STATE), 0.1)
    state_ssm_im = nrm((N_SSM_LAYERS, DEC_BATCH, SSM_GROUPS, SSM_STATE), 0.1)
    cache_cmp_kv = nrm((N_NSA_LAYERS, n_pool, PAGE_SIZE) + kv_row, 1.0)
    cache_slc_kv = nrm((N_NSA_LAYERS, n_pool, PAGE_SIZE) + kv_row, 1.0)
    cache_win_kv = nrm((N_NSA_LAYERS, DEC_BATCH, win_len) + kv_row, 1.0)
    cache_mem_kv = nrm((DEPTH, DEC_BATCH, N_MEM, MEM_HEADS, 2, MEM_HEAD_DIM), 1.0)
    return {
        'x_prompt': x_prompt,
        'x_sample': x_sample,
        'mem_prompt': mem_prompt,
        'state_ssm_re': state_ssm_re,
        'state_ssm_im': state_ssm_im,
        'cache_cmp_kv': cache_cmp_kv,
        'cache_slc_kv': cache_slc_kv,
        'cache_win_kv': cache_win_kv,
        'cache_mem_kv': cache_mem_kv,
        'page_table': page_table,
        'norm_mix_pre': 1.0 + nrm((DEPTH, D_MODEL), 0.05),
        'norm_mix_post': 1.0 + nrm((DEPTH, D_MODEL), 0.05),
        'norm_ffn_pre': 1.0 + nrm((DEPTH, D_MODEL), 0.05),
        'norm_ffn_post': 1.0 + nrm((DEPTH, D_MODEL), 0.05),
        'w_out': nrm((DEPTH, MIX_WIDTH, D_MODEL), MIX_WIDTH ** -0.5),
        'w_mem_kv': nrm((DEPTH, D_MODEL, MEM_HEADS * 2 * MEM_HEAD_DIM), D_MODEL ** -0.5),
        'w_ffn_in': nrm((DEPTH, D_MODEL, 2 * D_FF), D_MODEL ** -0.5),
        'w_ffn_out': nrm((DEPTH, D_FF, D_MODEL), D_FF ** -0.5),
        'ssm_w_in': nrm((N_SSM_LAYERS, D_MODEL, SSM_IN), D_MODEL ** -0.5),
        'ssm_a_re': -0.5 + nrm((N_SSM_LAYERS, SSM_GROUPS, SSM_STATE), 0.01),
        'ssm_a_im': ssm_a_im,
        'ssm_log_dt': ssm_log_dt,
        'ssm_b_re': nrm((N_SSM_LAYERS, SSM_GROUPS, SSM_STATE, SSM_GROUP), (2 * SSM_GROUP) ** -0.5),
        'ssm_b_im': nrm((N_SSM_LAYERS, SSM_GROUPS, SSM_STATE, SSM_GROUP), (2 * SSM_GROUP) ** -0.5),
        'ssm_c_re': nrm((N_SSM_LAYERS, SSM_GROUPS, SSM_GROUP, SSM_STATE), SSM_STATE ** -0.5),
        'ssm_c_im': nrm((N_SSM_LAYERS, SSM_GROUPS, SSM_GROUP, SSM_STATE), SSM_STATE ** -0.5),
        'ssm_d': nrm((N_SSM_LAYERS, SSM_WIDTH), 1.0),
        'ssm_w_glu': nrm((N_SSM_LAYERS, SSM_WIDTH, SSM_WIDTH), SSM_WIDTH ** -0.5),
        'ssm_b_glu': nrm((N_SSM_LAYERS, SSM_WIDTH), 0.01),
        'nsa_w_in': nrm((N_NSA_LAYERS, D_MODEL, NSA_IN), D_MODEL ** -0.5),
        'nsa_cmp_pe': nrm((N_NSA_LAYERS, CMP_BLOCK, 2, NSA_HEAD_DIM), 0.02),
        'nsa_cmp_w1': nrm((N_NSA_LAYERS, CMP_BLOCK, 2, NSA_HEAD_DIM, CMP_HIDDEN), (CMP_BLOCK * NSA_HEAD_DIM) ** -0.5),
        'nsa_cmp_b1': nrm((N_NSA_LAYERS, 2, CMP_HIDDEN), 0.01),
        'nsa_cmp_w2': nrm((N_NSA_LAYERS, 2, CMP_HIDDEN, NSA_HEAD_DIM), CMP_HIDDEN ** -0.5),
    }

def reference(x_prompt, x_sample, mem_prompt, state_ssm_re, state_ssm_im, cache_cmp_kv, cache_slc_kv,
              cache_win_kv, cache_mem_kv, page_table, norm_mix_pre, norm_mix_post, norm_ffn_pre, norm_ffn_post,
              w_out, w_mem_kv, w_ffn_in, w_ffn_out, ssm_w_in, ssm_a_re, ssm_a_im, ssm_log_dt, ssm_b_re, ssm_b_im,
              ssm_c_re, ssm_c_im, ssm_d, ssm_w_glu, ssm_b_glu, nsa_w_in, nsa_cmp_pe, nsa_cmp_w1, nsa_cmp_b1,
              nsa_cmp_w2):
    slopes = alibi_slopes()
    xp, xs = x_prompt, x_sample
    ssm_re_p, ssm_im_p, ssm_re_s, ssm_im_s = [], [], [], []
    cmp_p, slc_p, win_p, cmp_s, slc_s, win_s = [], [], [], [], [], []
    mem_p = []
    for i in range(DEPTH):
        j = i // N_MIXERS
        mkv_p = mem_kv_proj(mem_prompt, w_mem_kv[i])
        mem_p.append(mkv_p)
        mkv_s = cache_mem_kv[i]
        hp = rmsnorm(xp, norm_mix_pre[i])
        hs = rmsnorm(xs, norm_mix_pre[i])
        if i % N_MIXERS == 0:
            h0_p = jnp.zeros((xp.shape[0], SSM_GROUPS, SSM_STATE), jnp.complex64)
            h0_s = lax.complex(state_ssm_re[j].astype(F32), state_ssm_im[j].astype(F32))
            mp, hl_p = s5_mixer(hp, h0_p, mkv_p, ssm_w_in[j], ssm_a_re[j], ssm_a_im[j], ssm_log_dt[j], ssm_b_re[j],
                                ssm_b_im[j], ssm_c_re[j], ssm_c_im[j], ssm_d[j], ssm_w_glu[j], ssm_b_glu[j])
            ms, hl_s = s5_mixer(hs, h0_s, mkv_s, ssm_w_in[j], ssm_a_re[j], ssm_a_im[j], ssm_log_dt[j], ssm_b_re[j],
                                ssm_b_im[j], ssm_c_re[j], ssm_c_im[j], ssm_d[j], ssm_w_glu[j], ssm_b_glu[j])
            ssm_re_p.append(jnp.real(hl_p))
            ssm_im_p.append(jnp.imag(hl_p))
            ssm_re_s.append(jnp.real(hl_s))
            ssm_im_s.append(jnp.imag(hl_s))
        else:
            mp, (kc, ks, kw) = nsa_prompt(hp, mkv_p, nsa_w_in[j], nsa_cmp_pe[j], nsa_cmp_w1[j], nsa_cmp_b1[j],
                                          nsa_cmp_w2[j], slopes)
            ms, (sc, ss, sw) = nsa_sample(hs, mkv_s, cache_cmp_kv[j], cache_slc_kv[j], cache_win_kv[j], page_table,
                                          nsa_w_in[j], nsa_cmp_pe[j], nsa_cmp_w1[j], nsa_cmp_b1[j], nsa_cmp_w2[j],
                                          slopes)
            cmp_p.append(kc)
            slc_p.append(ks)
            win_p.append(kw)
            cmp_s.append(sc)
            slc_s.append(ss)
            win_s.append(sw)
        xp = xp + rmsnorm(mp @ w_out[i], norm_mix_post[i])
        xs = xs + rmsnorm(ms @ w_out[i], norm_mix_post[i])
        xp = xp + rmsnorm(swiglu_ffn(rmsnorm(xp, norm_ffn_pre[i]), w_ffn_in[i], w_ffn_out[i]), norm_ffn_post[i])
        xs = xs + rmsnorm(swiglu_ffn(rmsnorm(xs, norm_ffn_pre[i]), w_ffn_in[i], w_ffn_out[i]), norm_ffn_post[i])
    return (xp, xs, jnp.stack(ssm_re_p), jnp.stack(ssm_im_p), jnp.stack(ssm_re_s), jnp.stack(ssm_im_s),
            jnp.stack(cmp_p), jnp.stack(slc_p), jnp.stack(win_p), jnp.stack(cmp_s), jnp.stack(slc_s),
            jnp.stack(win_s), jnp.stack(mem_p))


_drawn_inputs = setup_inputs


def setup_inputs(seed=0):
    import zlib

    import numpy as np

    out = dict(_drawn_inputs(seed))
    spreads = {}
    factors = {'ssm_a_re': 3.887, 'ssm_b_glu': 8.0, 'nsa_cmp_pe': 5.369, 'nsa_cmp_b1': 8.0}
    for name, (base, spread) in spreads.items():
        noise = np.random.default_rng([zlib.crc32(name.encode()), seed]).standard_normal(out[name].shape)
        drawn = base * np.exp(spread * noise) if base else spread * noise
        out[name] = __import__('jax').numpy.asarray(drawn.astype(out[name].dtype))
    for name, factor in factors.items():
        out[name] = (out[name] * factor).astype(out[name].dtype)
    return out
```

```python
from contextlib import ExitStack

import concourse.bass as bass
from concourse import mybir
import numpy as np

F32 = mybir.dt.float32
I32 = mybir.dt.int32
ALU = mybir.AluOpType
ACT = mybir.ActivationFunctionType
AX_X = mybir.AxisListType.X
SP, POOL = mybir.EngineType.SP, mybir.EngineType.Pool

P = 128
D = 1024
KC = D // P
TP = 256
B = 8
TS = 4
T = TP + B * TS
FF = 2816
FC = FF // P
NMEM = 256
GRP = 48
SC = GRP // 2
SEG = 64
NSEG = TP // SEG
OCT = 8
NO = SC // OCT
H = 3
G = 4
PAGE = 128
NPG = 16
PG_STEP = 4
PAST = NPG * PAGE
NCMP = PAST // 16 - 1
NCP = TP // 16 - 1
WIN = 512
NROW = 128
NBLK = PAST // 64
NEG = -1e30
TAKEN = -1e30
EPS = 1e-6
SLOTS = 3
SLAB = 2048
SEQ_TAB = 2 * np.pi

N_MEM_SLAB, N_IN_SLAB, N_GLU_SLAB, N_OUT_SLAB, N_NSA_SLAB = 2, 4, 3, 4, 9
FI, FO = FC, 2 * KC

C1 = {"ident": (0, 128), "ones": (128, 256), "tau": (256, 320), "halfpi": (320, 321), "eps": (321, 322)}
C1N = 322
_c2 = [("causal", 384), ("cmask_d", 30), ("cmask_m", 30), ("cmp_d", NCMP), ("win_d", WIN), ("new_d", 32),
       ("slope", 3), ("gsel", 4), ("same", 128), ("earlier", 33 * 33), ("spread", 128)]
C2, _at = {}, 0
for _n, _w in _c2:
    C2[_n] = (_at, _at + _w)
    _at += _w
C2N = _at
_pr = [("norm", 8 * KC), ("a_re", SC), ("a_im", SC), ("log_dt", SC), ("h0", 2 * SC * B), ("d", 6), ("b_glu", 6),
       ("w2", 2 * 64), ("pe", 32), ("b1", 2)]
PR, _at = {}, 0
for _n, _w in _pr:
    PR[_n] = (_at, _at + _w)
    _at += _w
PRN = _at


class Banks:

    def __init__(self, full, free):
        self.full, self.free = full, free
        self.n_full, self.n_free = [0] * 8, [0] * 8
        self.uses = {}
        self.loop = None

    def begin_loop(self, trips, per):
        self.loop = (trips, dict(per), list(self.n_full), list(self.n_free))

    def end_loop(self):
        trips, per, full0, free0 = self.loop
        for b, k in per.items():
            assert self.n_full[b] - full0[b] == k
            self.n_full[b] = full0[b] + k * trips
            self.n_free[b] = free0[b] + k * trips
        self.loop = None

    def fill(self, pe, key, b, i=None):
        per = self.loop[1][b] if self.loop else 0
        before = self.n_free[b]
        if self.loop:
            pe.wait_ge(self.free[b], i * per + before)
        elif before:
            pe.wait_ge(self.free[b], before)
        self.n_full[b] += 1
        self.n_free[b] += 1
        self.uses[key] = (b, self.n_full[b], per, before)

    def filled(self, ins, key):
        ins.then_inc(self.full[self.uses[key][0]], 1)

    def _value(self, v, per, i):
        return v if not per or i is None else i * per + v

    def take(self, eng, key, i=None):
        b, v, per, _ = self.uses[key]
        eng.wait_ge(self.full[b], self._value(v, per, i))

    def give(self, ins, key):
        ins.then_inc(self.free[self.uses[key][0]], 1)

    def wait_given(self, eng, key, i=None):
        b, _, per, before = self.uses[key]
        eng.wait_ge(self.free[b], self._value(before + 1, per, i))

    def wait_former(self, eng, key, i=None):
        b, _, per, before = self.uses[key]
        if per and i is not None:
            eng.wait_ge(self.free[b], i * per + before)
        elif before:
            eng.wait_ge(self.free[b], before)


class Chain:

    def __init__(self, eng, sem):
        self.eng, self.sem, self.n, self.lp = eng, sem, 0, None

    def begin_loop(self, i, per):
        self.lp = (i, per, self.n)

    def end_loop(self, trips):
        i, per, n0 = self.lp
        assert self.n - n0 == per, self.n - n0
        self.n = n0 + per * trips
        self.lp = None

    def tick(self, ins):
        ins.then_inc(self.sem, 1)
        self.n += 1

    def sync(self):
        if self.lp:
            self.eng.wait_ge(self.sem, self.lp[0] * self.lp[1] + self.n)
        elif self.n:
            self.eng.wait_ge(self.sem, self.n)

    def step(self, ins):
        self.tick(ins)
        self.sync()


def trunk_kernel(nc, x_in, mem_in, cst1_in, cst2_in, slcd_in, prm_in, bmat_in, cmat_in, w8_in, wglu_in, wfi_in, wfo_in,
                 w1s_in, w1p_in, pages_in, cmp_in, slck_in, slcv_in, wink_in, winv_in, memk_in, memv_in, winold_in,
                 y_out, st_p_out, st_s_out, kv_out, winold_out, memkv_out):
    ctx = ExitStack()
    with ctx:
        def sb(name, n, dt=F32, parts=P):
            return ctx.enter_context(nc.sbuf_tensor(name, [parts, n], dt))

        def sem(name):
            return ctx.enter_context(nc.semaphore(name))

        X_ = sb("residual", KC * T)
        Hn_ = sb("normed", KC * T)
        Z_ = sb("projected", 17 * T)
        M_ = sb("mixed", KC * T)
        HID = sb("hidden", FC * T)
        W_ = sb("slabs", SLOTS * SLAB)
        AR = sb("arena", 12288)
        KV = sb("cmp_kv", 4 * H * NCMP + B * H * 64)
        U = sb("phase", 8704)
        XT = sb("phase_small", 2500)
        CS = sb("cst1", C1N)
        PRM = sb("params", PRN)
        SP5 = sb("s5_small", 13 * SC)
        RST = sb("rstd", T)
        STAT = sb("stats", 100)
        PT = sb("pages", P, I32, 1)

        X = X_[:, :].rearrange("p (k t) -> p k t", t=T)
        Hn = Hn_[:, :].rearrange("p (k t) -> p k t", t=T)
        Z = Z_[:, :].rearrange("p (k t) -> p k t", t=T)
        M = M_[:, :].rearrange("p (k t) -> p k t", t=T)
        HD = HID[:, :].rearrange("p (k t) -> p k t", t=T)
        W = W_[:, :].rearrange("p (s n) -> p s n", n=SLAB)

        def c1(name):
            a, b = C1[name]
            return CS[:, a:b]

        def c2(name):
            a, b = C2[name]
            return XT[:, a:b]

        def pr(name):
            a, b = PR[name]
            return PRM[:, a:b]

        ident, ones = c1("ident"), c1("ones")
        norm_g = pr("norm").rearrange("p (n k) -> p n k", k=KC)

        MEMT = M_[:, 0:KC * NMEM].rearrange("p (k t) -> p k t", t=NMEM)
        MK = AR[:, 0:4096].rearrange("p (b c n) -> p b c n", b=B, c=2)
        MV = AR[:, 4096:8192].rearrange("p (b t n) -> p b t n", b=B, t=2)
        MKV = AR[:, 8192:9216].rearrange("p (t n) -> p t n", t=2)
        MKT = AR[:, 9216:9728].rearrange("p (c n) -> p c n", c=2)
        QMB = AR[:, 9728:10752].rearrange("p (c b r) -> p c b r", c=2, b=B)
        MP = [AR[:, 10752 + 512 * j:11264 + 512 * j].rearrange("p (t n) -> p t n", t=2) for j in range(2)]
        MPT = AR[:, 11776:12288]
        PG = [AR[:, 6144 * s:6144 * s + 6144].rearrange("p (g c h s) -> p g c h s", g=NPG, c=16, h=H) for s in range(2)]
        BT = [HID[:, 3072 * r:3072 * r + 3072].rearrange("p (c n) -> p c n", n=P) for r in range(2)]
        R0 = Z_[:, 8 * T:8 * T + SC * SEG]
        R0S = Z_[:, 8 * T + SC * SEG:8 * T + SC * SEG + SC * B * TS]
        BX = [KV[:, 768 * r:768 * r + 768].rearrange("p (c j) -> p c j", j=32) for r in range(3)]
        BIN = [XT[:, 768 * r:768 * r + 768].rearrange("p (c j) -> p c j", j=32) for r in range(2)]
        W1S = U[:, 0:4096].rearrange("p (c a j f) -> p c a j f", c=2, a=2, j=8)
        COS = U[:, 4096:5632].rearrange("p (c t) -> p c t", t=SEG)
        SIN = U[:, 5632:7168].rearrange("p (c t) -> p c t", t=SEG)
        CM = [U[:, 7168 + 768 * r:7936 + 768 * r].rearrange("p (c j) -> p c j", j=32) for r in range(2)]
        S5W = [Hn_[:, 1024 * r:1024 * r + 1024] for r in range(2)]
        S5T = M_[:, 0:512]
        S5H = [XT[:, 1024 * r:1024 * r + 1024] for r in range(2)]
        S5G = M_[:, 512:1536]
        KCT = KV[:, 0:4 * H * NCMP].rearrange("p (b n) -> p b n", b=4)
        VC = KV[:, 4 * H * NCMP:].rearrange("p (b n) -> p b n", b=B)
        HCMP = [sb("cmp_hidden", H * NCMP)[:, :], XT[:, 2048:2048 + H * NCMP]]

        W1P = U[:, 0:4096].rearrange("p (a j f) -> p a j f", a=2, j=16)
        PTC = HID[:, 0:3072].rearrange("p (g q) -> p g q", q=TP)
        SU = [HID[:, 3072 + 768 * r:3840 + 768 * r].rearrange("p (g n) -> p g n", g=2) for r in range(2)]
        KD = HID[:, 4608:6144].rearrange("p (j n) -> p j n", n=TP)
        VT = Hn_[:, 0:768].rearrange("p (t j e) -> p t j e", t=2, e=64)
        PTU = [Hn_[:, 768 + 768 * r:1536 + 768 * r].rearrange("p (g n) -> p g n", g=2) for r in range(2)]
        SCP = pr("h0")[:, 0:2 * 12 * NCP].rearrange("p (t g n) -> p t g n", t=2, n=NCP)
        HCP = SP5[:, 0:2 * H * NCP].rearrange("p (c n) -> p c n", c=2)
        VCP = SP5[:, 96:96 + H * 64]
        KCP = CS[:, 256:256 + H * NCP]
        MISC = HCMP[0]
        GP = MISC[:, 0:72].rearrange("p (t n) -> p t n", t=2)
        GS = MISC[:, 72:108]
        GR = MISC[:, 108:117]
        CMX, CSM = MISC[:, 120:144], MISC[:, 144:168]
        NM, RS, RW = [STAT[:, 80:84], STAT[:, 84:88]], [STAT[:, 88:92], STAT[:, 92:96]], MISC[:, 168:172]
        IMP = MISC[:, 180:279].rearrange("p (h j) -> p h j", h=H)
        MS = MISC[:, 279:378].rearrange("p (h j) -> p h j", h=H)
        NEWMAX = MISC[:, 120:123]
        NS, SS = STAT[:, 60:69], STAT[:, 69:78]
        QBD = U[:, 8288:8672].rearrange("p (b h r) -> p b h r", b=4, h=H)
        Q0 = Hn_[:, 384:768].rearrange("p (h r) -> p h r", h=H)
        VN = Hn_[:, 768:1152].rearrange("p (j e) -> p j e", e=64)
        PC = Hn_[:, 1152:1536].rearrange("p (h n) -> p h n", h=H)
        PTN = Hn_[:, 1536:1920]
        PCT = Hn_[:, 1920:2304]
        GT = HID[:, 6200:6236].rearrange("p (n g) -> p n g", g=G)
        SW = HID[:, 0:3 * 544].rearrange("p (h n) -> p h n", h=H)
        PTW = HID[:, 1632:3168].rearrange("p (t n) -> p t n", t=4)
        S_SLC = U[:, 0:3 * 2080].rearrange("p (h n) -> p h n", h=H)
        TOP = MISC[:, 172:180]
        SO = Hn_[:, 0:768].rearrange("p (c n) -> p c n", c=4)
        SNEW = HID[:, 6240:6336].rearrange("p (h n) -> p h n", h=H)
        PTS = HID[:, 0:6144]
        SLCD = U[:, 6240:6240 + PAST]
        WK = AR[:, 0:6144].rearrange("p (b h n) -> p b h n", b=4, h=H)
        WV = AR[:, 6144:12288].rearrange("p (b t n) -> p b t n", b=B, t=4)
        KP = [AR[:, 6144 * s:6144 * s + 6144].rearrange("p (g h n) -> p g h n", g=NPG, h=H) for s in range(2)]
        VAL = [AR[:, 3072 * s:3072 * s + 3072] for s in range(4)] + [U[:, 3072 * s:3072 * s + 3072] for s in range(2)]
        VP = [x.rearrange("p (g n) -> p g n", g=NPG) for x in VAL]

        BK = [ctx.enter_context(nc.psum_tensor(f"bank{b}", [P, 512], F32)) for b in range(8)]
        banks = Banks([sem(f"bank{b}_full") for b in range(8)], [sem(f"bank{b}_free") for b in range(8)])

        x_loaded, cst_loaded, prm_loaded, smat_loaded = sem("x_loaded"), sem("cst_loaded"), sem("prm_loaded"), sem("smat_loaded")
        memt_loaded, mkv_loaded, w1_loaded = sem("memt_loaded"), sem("mkv_loaded"), sem("w1_loaded")
        slab_loaded = [sem(f"slab{s}_loaded") for s in range(SLOTS)]
        page_loaded = [sem(f"pages{s}_loaded") for s in range(2)]
        pages_used = sem("pages_used")
        half_used = sem("half_slab_used")
        sq_done, ms_done, rt_done, h_done, x_done = sem("squares_done"), sem("meansq_done"), sem("root_done"), sem("normed_done"), sem("residual_done")
        sil_done = sem("silu_done")
        dve_seq, act_seq, pool_seq = sem("dve_steps"), sem("act_steps"), sem("pool_steps")
        bx_done = sem("s5_input_matrix_done")
        trig_arg, trig_done = sem("angles_done"), sem("trig_done")
        dt_done = sem("s5_exp_in"), sem("s5_exp_out")
        scanned, h5_done = sem("s5_scanned"), sem("s5_states_done")
        carry0 = sem("s5_carry_cleared")
        glu_in, bt_cleared = sem("glu_in_ready"), sem("s5_blocks_cleared")
        mix_done = sem("mixed_done")
        nmax_done, prob_done, qmb_done = sem("mem_max_done"), sem("mem_prob_done"), sem("mem_query_blocks")
        memkv_stored, state_stored = sem("mem_kv_stored"), sem("state_stored")
        stored, pt_loaded = sem("stored"), sem("page_table_loaded")

        slcd_loaded = sem("distances_loaded")
        cst2_loaded, w1p_loaded, win_loaded = sem("cst2_loaded"), sem("w1p_loaded"), sem("win_loaded")
        kpage_loaded = [[sem(f"key_pages{s}_{c}_loaded") for c in range(2)] for s in range(2)]
        vpage_loaded = [sem(f"value_pages{s}_loaded") for s in range(6)]
        win_used = sem("window_values_used")
        kv_stored, kd_done, kept = sem("kv_stored"), sem("prompt_keys_copied"), sem("slc_values_used")
        cp_scored, cp_exp, cp_prob = sem("prompt_cmp_scored"), sem("prompt_cmp_exp"), sem("prompt_cmp_prob")
        u_max, u_exp, u_prob = sem("unit_max"), sem("unit_exp"), sem("unit_prob")
        qbd_done, q_done, row_gates = sem("sample_query_blocks"), sem("sample_queries"), sem("sample_row_gates")
        sc_max, sc_exp, sc_prob = sem("sample_cmp_max"), sem("sample_cmp_exp"), sem("sample_cmp_prob")
        imp_done = sem("importance_done")
        sw_max, sw_exp, sw_prob = sem("sample_win_max"), sem("sample_win_exp"), sem("sample_win_prob")
        ss_max, ss_exp, ss_prob = sem("sample_slc_max"), sem("sample_slc_exp"), sem("sample_slc_prob")

        def page_numbers(eng, which, b, i, pool_in):
            at = PT[0:1, bass.ds(i * PG_STEP + b * NPG, PG_STEP)]
            return nc.values_load_multi_w_load_instructions(at, engines=[which], min_val=0, max_val=pool_in.shape[0] - 1)[1]

        def page(pool_in, r):
            return pool_in[bass.ds(r, 1), :, :].rearrange("a p n -> p (a n)")

        def load_key_pages(eng, which, b, s):
            with eng.Fori(0, NPG // PG_STEP) as i:
                for u, r in enumerate(page_numbers(eng, which, b, i, slck_in)):
                    lo = 64 * (b % 2)
                    dst = AR[lo:lo + 64, bass.ds(i * (384 * PG_STEP) + (6144 * s + 384 * u), 384)]
                    eng.dma_start(dst, page(slck_in, r)).then_inc(kpage_loaded[s][b % 2], 16)

        def load_value_pages(eng, which, b):
            s = b % 6
            with eng.Fori(0, NPG // PG_STEP) as i:
                for u, r in enumerate(page_numbers(eng, which, b, i, slcv_in)):
                    dst = VAL[s][:, bass.ds(i * (192 * PG_STEP) + 192 * u, 192)]
                    eng.dma_start(dst, page(slcv_in, r)).then_inc(vpage_loaded[s], 16)

        def wait_value_slot(eng, b):
            if b < 2:
                for h in range(H):
                    banks.take(eng, ("sws", h))
            elif b < 4:
                eng.wait_ge(win_used, 1)
            elif b < 6:
                banks.take(eng, ("st", NPG))
            else:
                eng.wait_ge(kept, 1)

        released = {}

        def slab_ready(pe, n, i=None, per=0):
            v = 16 * (n // SLOTS + 1)
            pe.wait_ge(slab_loaded[n % SLOTS], v if i is None else i * (16 * per // SLOTS) + v)

        def release(n, key=None, half=None):
            if key is not None:
                b, v, per, _ = banks.uses[key]
                released[n] = (banks.full[b], v, per)
            else:
                released[n] = half

        FIRST = {}
        n = 0
        for l in range(2):
            FIRST["mem", l] = n
            n += N_MEM_SLAB
            if l == 0:
                FIRST["in", l] = n
                n += N_IN_SLAB
                FIRST["glu", l] = n
                n += N_GLU_SLAB
            else:
                FIRST["in", l] = n
                n += N_NSA_SLAB
            FIRST["out", l] = n
            n += N_OUT_SLAB
            FIRST["fi", l] = n
            n += FI
            FIRST["fo", l] = n
            n += FO
        block = ctx.enter_context(nc.Block())
        sq_count = lambda norm: 8 * norm

        @block.tensor
        def _(pe):
            turn = [0]

            def next_bank():
                turn[0] = (turn[0] + 1) % 4
                return turn[0]

            def slab2(n, i=None):
                return W[:, n % SLOTS, :]

            def norm_chunk(norm, m):
                if m == 0:
                    banks.fill(pe, ("norm", norm), 7)
                pe.wait_ge(sq_done, 8 * norm + m + 1)
                ins = nc.tensor.matmul(BK[7][:, 0:T], ones, Hn[:, m, :], start=(m == 0), stop=(m == 7))
                if m == 7:
                    banks.filled(ins, ("norm", norm))

            def gemm(name, l, rhs, kc, slabs, width, post=None, ready=None, extra=None):
                m = 0
                for s in range(slabs):
                    n = FIRST[name, l] + s
                    slab_ready(pe, n)
                    wt = slab2(n)[:, 0:kc * 256].rearrange("p (k n) -> p k n", n=256)
                    for c in range(2):
                        if m >= width:
                            key = extra(wt)
                            break
                        key = (name, l, m)
                        b = next_bank()
                        banks.fill(pe, key, b)
                        for k in range(kc):
                            if m == 0 and ready:
                                ready(k)
                            ins = nc.tensor.matmul(BK[b][:, 0:T], wt[:, k, c * P:c * P + P], rhs[:, k, :],
                                                   start=(k == 0), stop=(k == kc - 1))
                        banks.filled(ins, key)
                        if post:
                            post(m)
                        m += 1
                    release(n, key)

            def mem_project(l):
                pe.wait_ge(memt_loaded, 16 * (l + 1))
                for s in range(N_MEM_SLAB):
                    n = FIRST["mem", l] + s
                    slab_ready(pe, n)
                    wt = slab2(n).rearrange("p (k n) -> p k n", n=256)
                    for t in range(2):
                        b = next_bank()
                        key = ("memkv", l, s, t)
                        banks.fill(pe, key, b)
                        for k in range(KC):
                            ins = nc.tensor.matmul(BK[b][:, 0:256], MEMT[:, k, t * P:t * P + P], wt[:, k, :],
                                                   start=(k == 0), stop=(k == KC - 1))
                        banks.filled(ins, key)
                    release(n, key)
                b = next_bank()
                banks.fill(pe, ("memkT", l), b)
                for s in range(N_MEM_SLAB):
                    for t in range(2):
                        banks.wait_given(pe, ("memkv", l, s, t))
                for c in range(2):
                    for t in range(2):
                        ins = nc.tensor.transpose(BK[b][:, 256 * c + P * t:256 * c + P * t + P],
                                                  MKV[:, t, 256 * c:256 * c + P], ident)
                banks.filled(ins, ("memkT", l))

            def mem_attend(l, zq):
                banks.wait_given(pe, ("memkT", l))
                for hd in range(4):
                    c, r = hd // 2, 64 * (hd % 2)
                    key = ("ms", l, hd)
                    b = 0 + hd % 2
                    banks.wait_given(pe, (("in", l, zq + c)))
                    banks.fill(pe, key, b)
                    for t in range(2):
                        ins = nc.tensor.matmul(BK[b][:, 256 * t:256 * t + 256], Z[r:r + 64, zq + c, t * P:t * P + P],
                                               MKT[r:r + 64, c, :], start=True, stop=True)
                    banks.filled(ins, key)
                    if hd >= 1:
                        mem_pv(l, hd - 1)
                mem_pv(l, 3)
                pe.wait_ge(qmb_done, l + 1)
                pe.wait_ge(mkv_loaded, 16 * 2 * (l + 1))
                banks.fill(pe, ("ms", l, 4), 0)
                for b in range(B):
                    for c in range(2):
                        ins = nc.tensor.matmul(BK[0][64 * c:64 * c + 64, 0:256], QMB[:, c, b, :], MK[:, b, c, :],
                                               start=(b == 0), stop=(b == B - 1))
                banks.filled(ins, ("ms", l, 4))
                pe.wait_ge(prob_done, 5 * l + 5)
                banks.fill(pe, ("mt", l, 4), 2)
                for t in range(2):
                    ins = nc.tensor.transpose(BK[2][:, P * t:P * t + P], MP[0][:, 0, P * t:P * t + P], ident)
                banks.filled(ins, ("mt", l, 4))
                banks.wait_given(pe, ("mt", l, 4))
                banks.fill(pe, ("mo", l, 2), 3)
                for c in range(2):
                    for b in range(B):
                        for t in range(2):
                            ins = nc.tensor.matmul(BK[3][:, 64 * c + 8 * b:64 * c + 8 * b + 8],
                                                   MV[:, b, t, P * c:P * c + P],
                                                   MPT[:, P * t + 64 * c + 8 * b:P * t + 64 * c + 8 * b + 8],
                                                   start=(t == 0), stop=(t == 1))
                banks.filled(ins, ("mo", l, 2))

            def mem_pv(l, hd):
                c, r = hd // 2, 64 * (hd % 2)
                pe.wait_ge(prob_done, 5 * l + hd + 1)
                banks.fill(pe, ("mt", l, hd), 2)
                for mt in range(2):
                    for t in range(2):
                        ins = nc.tensor.transpose(BK[2][:, 256 * mt + P * t:256 * mt + P * t + P],
                                                  MP[hd % 2][:, t, P * mt:P * mt + P], ident)
                banks.filled(ins, ("mt", l, hd))
                banks.wait_given(pe, ("mt", l, hd))
                key = ("mo", l, c)
                if hd % 2 == 0:
                    banks.fill(pe, key, 3)
                for mt in range(2):
                    ins = nc.tensor.matmul(BK[3][r:r + 64, 0:256], MKV[:, mt, 256 * c + P + r:256 * c + P + r + 64],
                                           MPT[:, 256 * mt:256 * mt + 256], start=(mt == 0), stop=(mt == 1))
                if hd % 2 == 1:
                    banks.filled(ins, key)

            def s5_blocks():
                pe.wait_ge(bx_done, 2)
                for r in range(2):
                    v = BX[r].rearrange("p (k q) j -> p k (q j)", q=4)
                    for part in range(2):
                        key = ("bt", r, part)
                        b = 4 + (2 * r + part) % 2
                        banks.fill(pe, key, b)
                        for k in range(4 * part, min(4 * part + 4, 6)):
                            ins = nc.tensor.transpose(BK[b][:, P * (k % 4):P * (k % 4) + P], v[:, k, :], ident)
                        banks.filled(ins, key)

            def cmp_bias():
                pe.wait_ge(w1_loaded, 16)
                banks.fill(pe, "pe", 6)
                for c in range(2):
                    for a in range(2):
                        for j in range(8):
                            q = 16 * c + 8 * a + j
                            ins = nc.tensor.matmul(BK[6][:, c:c + 1], W1S[:, c, a, j, :], pr("pe")[:, q:q + 1],
                                                   start=(a + j == 0), stop=(a * 8 + j == 15))
                banks.filled(ins, "pe")

            def s5_in(o, tok, key, width, i=None):
                for r in range(2):
                    banks.fill(pe, key + ("re", "im")[r], r, i)
                    for cc in range(OCT):
                        c = OCT * o + cc
                        ins = nc.tensor.matmul(BK[r][:, cc * width:cc * width + width], BT[r][:, c, :], tok(c // 4),
                                               start=True, stop=True)
                    banks.filled(ins, key + ("re", "im")[r])

            def s5_y(o, key, width, seen, i=None):
                pe.wait_ge(h5_done, seen)
                banks.fill(pe, key, 4, i)
                hb = S5H[o % 2]
                for cc in range(OCT):
                    c, ku, q = OCT * o + cc, cc // 4, cc % 4
                    for r in range(2):
                        ins = nc.tensor.matmul(BK[4][32 * q:32 * q + 32, ku * width:ku * width + width], CM[r][:, c, :],
                                               hb[:, 512 * r + cc * width:512 * r + cc * width + width],
                                               start=(r == 0), stop=(r == 1))
                banks.filled(ins, key)

            def compress(u, c, i):
                key = ("hc", u, c)
                banks.fill(pe, key, 5 + c, i)
                if c == 0:
                    pe.wait_ge(page_loaded[u], i * (16 * NPG) + 16 * NPG)
                for a in range(2):
                    for j in range(8):
                        out = BK[5 + c][:, 0:387].rearrange("p (h n) -> p h n", n=129)[:, :, 1 - a:129 - a]
                        ins = nc.tensor.matmul(out.rearrange("p h (g s) -> p h g s", s=8), W1S[:, c, a, j, :],
                                               PG[u][:, :, c * 8 + j, :, :].rearrange("p g h s -> p h g s"),
                                               start=(a + j == 0), stop=(a * 8 + j == 15), skip_group_check=True)
                banks.filled(ins, key)

            def compress_k(u, i):
                banks.fill(pe, ("ck", u), 7, i)
                banks.wait_given(pe, ("hc", u, 0), i)
                ins = nc.tensor.matmul(BK[7][64 * u:64 * u + 64, 0:H * NCMP], pr("w2")[:, 0:64], HCMP[0],
                                       start=True, stop=True)
                banks.filled(ins, ("ck", u))

            def compress_v(u, i):
                banks.fill(pe, ("cv", u), 7, i)
                banks.wait_given(pe, ("hc", u, 1), i)
                for h in range(H):
                    ins = nc.tensor.matmul(BK[7][0:NCMP, 64 * h:64 * h + 64], HCMP[1][:, NCMP * h:NCMP * h + NCMP],
                                           pr("w2")[:, 64:128], start=True, stop=True)
                banks.filled(ins, ("cv", u))

            def channel_mixer(l):
                n0 = FIRST["fi", l]

                def fi_step(u, i=None):
                    n = n0 + u
                    slab_ready(pe, n, i, SLOTS)
                    wt = slab2(n).rearrange("p (k n) -> p k n", n=256)
                    for c in range(2):
                        key = ("fi", l, u if i is not None else "last", c)
                        banks.fill(pe, key, 2 * (u % SLOTS) + c, i)
                        for k in range(KC):
                            ins = nc.tensor.matmul(BK[2 * (u % SLOTS) + c][:, 0:T], wt[:, k, c * P:c * P + P],
                                                   Hn[:, k, :], start=(k == 0), stop=(k == KC - 1))
                        banks.filled(ins, key)
                    if i is not None:
                        release(n, key)
                    else:
                        release(n0 + FI - 1, key)

                pe.wait_ge(h_done, 8 * (2 * l + 2))
                banks.begin_loop(FI // SLOTS, {b: 1 for b in range(2 * SLOTS)})
                with pe.Fori(0, FI // SLOTS) as i:
                    for u in range(SLOTS):
                        fi_step(u, i)
                banks.end_loop()
                for u in range(FI // SLOTS * SLOTS, FI):
                    fi_step(u)
                for u in range(SLOTS):
                    banks.wait_given(pe, ("fi", l, u, 1), FI // SLOTS - 1)
                banks.wait_given(pe, ("fi", l, "last", 1))
                n0 = FIRST["fo", l]
                for m in range(KC):
                    key = ("fo", l, m)
                    b = m % 2
                    banks.fill(pe, key, b)
                    for kh in range(2):
                        n = n0 + 2 * m + kh
                        slab_ready(pe, n)
                        wt = slab2(n)[:, 0:11 * P].rearrange("p (k n) -> p k n", n=P)
                        for k in range(11):
                            ins = nc.tensor.matmul(BK[b][:, 0:T], wt[:, k, :], HD[:, 11 * kh + k, :],
                                                   start=(kh + k == 0), stop=(kh * 11 + k == 21))
                        if kh == 0:
                            ins.then_inc(half_used, 1)
                            release(n, half=(half_used, KC * l + m + 1, 0))
                    banks.filled(ins, key)
                    release(n, key)
                    if m:
                        norm_chunk(4 * l + 3, m - 1)
                norm_chunk(4 * l + 3, KC - 1)

            pe.wait_ge(cst_loaded, 16)
            pe.wait_ge(prm_loaded, 16)
            for m in range(KC):
                norm_chunk(0, m)
            mem_project(0)
            gemm("in", 0, Hn, KC, N_IN_SLAB, 8, ready=lambda k: pe.wait_ge(h_done, k + 1))
            cmp_bias()
            s5_blocks()
            mem_attend(0, 6)
            for r in range(2):
                for part in range(2):
                    banks.wait_given(pe, ("bt", r, part))
            for m in range(4, 8):
                banks.wait_given(pe, ("in", 0, m))
            pe.wait_ge(smat_loaded, 32)
            banks.begin_loop(4, {0: 3, 1: 3, 4: 3, 5: 2, 6: 2, 7: 4})
            with pe.Fori(0, 4) as i:
                def tok(k):
                    return Z[:, k, bass.ds(i * SEG, SEG)]
                for o in range(NO):
                    s5_in(o, tok, f"s5{o}", SEG, i)
                    u, c = [(0, 0), (0, 1), (1, 0)][o]
                    compress(u, c, i)
                    if o == 1:
                        compress_k(0, i)
                    if o == 2:
                        compress_v(0, i)
                    s5_y(o, f"y{o}", SEG, i * 3 + o + 1, i)
                compress(1, 1, i)
                compress_k(1, i)
                compress_v(1, i)
            banks.end_loop()
            for o in range(NO + 1):
                if o < NO:
                    s5_in(o, lambda k: Z[:, k, TP:T], f"t5{o}", B * TS)
                if o:
                    s5_y(o - 1, f"u{o - 1}", B * TS, NSEG * NO + o)
            gemm("glu", 0, Z, 6, N_GLU_SLAB, 6, ready=lambda k: pe.wait_ge(glu_in, k + 1))

            def post(norm):
                return lambda m: norm_chunk(norm, m - 1) if m else None

            for c in range(3):
                banks.wait_given(pe, ("mo", 0, c))
            gemm("out", 0, M, KC, N_OUT_SLAB, KC, post=post(1), ready=lambda k: pe.wait_ge(mix_done, k + 1) if k < 6 else None)
            norm_chunk(1, 7)
            for m in range(KC):
                norm_chunk(2, m)
            channel_mixer(0)

            def gates(wt):
                key = "gates"
                b = next_bank()
                banks.fill(pe, key, b)
                for j, (t0, n) in enumerate(((0, P), (P, P), (TP, B * TS))):
                    for k in range(KC):
                        ins = nc.tensor.matmul(BK[b][0:n, 36 * j:36 * j + 36], Hn[:, k, t0:t0 + n], wt[:, k, P:P + 36],
                                               start=(k == 0), stop=(k == KC - 1))
                banks.filled(ins, key)
                return key

            mem_project(1)
            for m in range(KC):
                norm_chunk(4, m)
            gemm("in", 1, Hn, KC, N_NSA_SLAB, 17, ready=lambda k: pe.wait_ge(h_done, 16 + k + 1), extra=gates)
            mem_attend(1, 15)
            for m in range(12, 17):
                banks.wait_given(pe, ("in", 1, m))
            pe.wait_ge(cst2_loaded, 16)
            banks.wait_given(pe, "gates")
            banks.fill(pe, "rowgates", 4)
            banks.filled(nc.tensor.matmul(BK[4][:, 0:36], c2("spread")[0:32, :], GS[0:32, :], start=True, stop=True), "rowgates")
            pe.wait_ge(w1p_loaded, 16)
            for c in range(2):
                banks.fill(pe, ("pc", c), 5 + c)
            for a in range(2):
                for j in range(16):
                    for c in range(2):
                        rows = Z[64 * c:64 * c + 64, 6:9, 16 * a + j:16 * a + j + 16 * NCP - 15:16]
                        ins = nc.tensor.matmul(BK[5 + c][:, 0:H * NCP].rearrange("p (h n) -> p h n", h=H),
                                               W1P[64 * c:64 * c + 64, a, j, :], rows,
                                               start=(a + j == 0), stop=(a * 16 + j == 31))
                        if a * 16 + j == 31:
                            banks.filled(ins, ("pc", c))
            for b3 in range(3):
                key = ("vt", b3)
                banks.fill(pe, key, b3)
                for jj in range(2):
                    for t in range(2):
                        ins = nc.tensor.transpose(BK[b3][:, P * (2 * t + jj):P * (2 * t + jj) + P],
                                                  Z[:, 9 + 2 * b3 + jj, t * P:t * P + P], ident)
                banks.filled(ins, key)
            banks.wait_given(pe, ("pc", 0))
            banks.fill(pe, "pck", 3)
            for r in range(2):
                ins = nc.tensor.matmul(BK[3][64 * r:64 * r + 64, 0:H * NCP], pr("w2")[:, 0:64], HCP[:, 0, :], start=True, stop=True)
            banks.filled(ins, "pck")
            banks.wait_given(pe, ("pc", 1))
            banks.fill(pe, "pcv", 4)
            for h in range(H):
                ins = nc.tensor.matmul(BK[4][0:NCP, 64 * h:64 * h + 64], HCP[:, 1, NCP * h:NCP * h + NCP], pr("w2")[:, 64:128],
                                       start=True, stop=True)
            banks.filled(ins, "pcv")
            banks.wait_given(pe, "pck")
            for par in range(2):
                banks.fill(pe, ("pcs", par), 5 + par)
            for t in range(2):
                for h in range(H):
                    for gg in range(2):
                        n = (t * H + h) * 2 + gg
                        for par in range(2):
                            r = 64 * par
                            ins = nc.tensor.matmul(BK[5 + par][:, NCP * n:NCP * n + NCP], Z[r:r + 64, 2 * h + gg, t * P:t * P + P],
                                                   KCP[r:r + 64, NCP * h:NCP * h + NCP], start=True, stop=True)
                            if n == 11:
                                banks.filled(ins, ("pcs", par))
            pe.wait_ge(cp_prob, 1)
            for n in range(6):
                key = ("pct", n)
                banks.fill(pe, key, 5 + n % 2)
                for g in range(2):
                    for t in range(2):
                        ins = nc.tensor.transpose(BK[5 + n % 2][0:NCP, 256 * g + P * t:256 * g + P * t + P],
                                                  SCP[:, t, 2 * n + g, :], ident)
                banks.filled(ins, key)
            for n in range(6):
                banks.wait_given(pe, ("pct", n))
            for n in range(3):
                banks.wait_given(pe, ("vt", n))
            banks.wait_given(pe, "pcv")
            pe.wait_ge(kd_done, 1)

            def unit_scores(n):
                h, par, br = n // 4, n // 2 % 2, n % 2
                r = 64 * par
                keys = Z[0:64, 9 + 3 * br + h, 0:TP] if par == 0 else KD[64:128, 3 * br + h, :]
                for gg in range(2):
                    key = ("us", n, gg)
                    b = 2 * (n % 2) + gg
                    banks.fill(pe, key, b)
                    nc.tensor.matmul(BK[b][:, 0:P], Z[r:r + 64, 2 * h + gg, 0:P], keys[:, 0:P], start=True, stop=True)
                    banks.filled(nc.tensor.matmul(BK[b][:, P:P + TP], Z[r:r + 64, 2 * h + gg, P:TP], keys, start=True, stop=True), key)

            def unit_turn(n):
                pe.wait_ge(u_prob, n + 1)
                for gg in range(2):
                    key = ("ut", n, gg)
                    banks.fill(pe, key, 4 + gg)
                    for j in range(3):
                        ins = nc.tensor.transpose(BK[4 + gg][:, P * j:P * j + P], SU[n % 2][:, gg, P * j:P * j + P], ident)
                    banks.filled(ins, key)

            def unit_pv(n):
                h, par, br = n // 4, n // 2 % 2, n % 2
                r = 64 * par
                if n % 4 == 0:
                    banks.fill(pe, ("po", h), 6)
                if br == 0:
                    for gg in range(2):
                        nc.tensor.matmul(BK[6][r:r + 64, TP * gg:TP * gg + TP], VCP[0:NCP, 64 * h:64 * h + 64],
                                         PTC[0:NCP, 4 * h + par + 2 * gg, :], start=(gg == 0), stop=False, skip_group_check=True)
                for gg in range(2):
                    banks.wait_given(pe, ("ut", n, gg))
                    nc.tensor.matmul(BK[6][r:r + 64, TP * gg:TP * gg + TP], VT[:, 0, 3 * br + h, :], PTU[n % 2][:, gg, 0:TP],
                                     start=False, stop=False, skip_group_check=True)
                    ins = nc.tensor.matmul(BK[6][r:r + 64, TP * gg + P:TP * gg + TP], VT[:, 1, 3 * br + h, :],
                                           PTU[n % 2][:, gg, TP:TP + P], start=False, stop=(br == 1), skip_group_check=True)
                if n % 4 == 3:
                    banks.filled(ins, ("po", h))

            def page_scores(step):
                b, c, h = step // 12, step // 3 % 4, step % 3
                if step % 12 == 0:
                    if b == 0:
                        pe.wait_ge(qbd_done, 1)
                    for parity in range(2):
                        pe.wait_ge(kpage_loaded[b % 2][parity], 256 * (b // 2 + 1))
                banks.fill(pe, ("sk", step), 7)
                ins = nc.tensor.matmul(BK[7][32 * b:32 * b + 32, :].rearrange("p (g n) -> p g n", n=P), QBD[:, b, h, :],
                                       KP[b % 2][:, 4 * c:4 * c + 4, h, :], start=True, stop=True)
                banks.filled(ins, ("sk", step))

            unit_scores(0)
            for n in range(14):
                more = iter(range(4 * (n - 2), 4 * (n - 1)) if n >= 2 else ())
                if n < 11:
                    unit_scores(n + 1)
                if n >= 2:
                    page_scores(next(more))
                if 1 <= n < 13:
                    unit_turn(n - 1)
                if n >= 2:
                    page_scores(next(more))
                    unit_pv(n - 2)
                for step in more:
                    page_scores(step)
            for j3 in range(2):
                key = ("vn", j3)
                banks.fill(pe, key, 4 + j3)
                for j in range(3):
                    ins = nc.tensor.transpose(BK[4 + j3][0:32, P * j:P * j + P], Z[:, 9 + 3 * j3 + j, TP:T], ident)
                banks.filled(ins, key)
            pe.wait_ge(q_done, 1)
            banks.fill(pe, "snew", 0)
            for j in range(6):
                ins = nc.tensor.matmul(BK[0][:, 32 * j:32 * j + 32], Q0[0:64, j % 3, :], Z[0:64, 9 + j, TP:T], start=True, stop=True)
            banks.filled(ins, "snew")
            banks.fill(pe, "scs", 1)
            for h in range(H):
                for b in range(4):
                    ins = nc.tensor.matmul(BK[1][32 * b:32 * b + 32, P * h:P * h + NCMP], QBD[:, b, h, :],
                                           KCT[:, b, NCMP * h:NCMP * h + NCMP], start=True, stop=True)
            banks.filled(ins, "scs")
            pe.wait_ge(win_loaded, 16 * 5)
            for h in range(H):
                key = ("sws", h)
                banks.fill(pe, key, (2, 3, 4)[h])
                for b in range(4):
                    ins = nc.tensor.matmul(BK[(2, 3, 4)[h]][32 * b:32 * b + 32, :], QBD[:, b, h, :], WK[:, b, h, :],
                                           start=True, stop=True)
                banks.filled(ins, key)
            pe.wait_ge(imp_done, 1)
            banks.fill(pe, "imp", 5)
            banks.filled(nc.tensor.matmul(BK[5][:, 0:96], c2("same"), IMP[:, :, 0:32], start=True, stop=True), "imp")
            pe.wait_ge(sc_prob, 1)
            banks.wait_given(pe, "imp")
            banks.fill(pe, "sct", 5)
            for h in range(H):
                ins = nc.tensor.transpose(BK[5][0:NCMP, P * h:P * h + P], PC[:, h, 0:NCMP], ident)
            banks.filled(ins, "sct")
            pe.wait_ge(sw_prob, 1)
            for t in range(5):
                key = ("swt", t)
                banks.fill(pe, key, t % 4)
                for h in range(H):
                    if t < 4:
                        ins = nc.tensor.transpose(BK[t % 4][:, P * h:P * h + P], SW[:, h, P * t:P * t + P], ident)
                    else:
                        ins = nc.tensor.transpose(BK[t % 4][0:32, P * h:P * h + P], SW[:, h, WIN:WIN + 32], ident)
                banks.filled(ins, key)
            for j3 in range(2):
                banks.wait_given(pe, ("vn", j3))
            banks.fill(pe, "so0", 6)
            banks.fill(pe, "so1", 7)

            def seq_pv(b, probs, values, first=False, last=False):
                r = 64 * (b % 2)
                out = BK[6 + b // 4][r:r + 48, 192 * (b // 2 % 2):192 * (b // 2 % 2) + 192]
                return nc.tensor.matmul(out, probs[:, 48 * b:48 * b + 48], values, start=first, stop=last, skip_group_check=True)
            banks.wait_given(pe, "sct")
            for b in range(B):
                seq_pv(b, PCT[0:NCMP, :], VC[0:NCMP, b, :], first=b // 2 % 2 == 0)
            for t in range(5):
                banks.wait_given(pe, ("swt", t))
            for b in range(B):
                seq_pv(b, PTN[0:32, :], VN[0:32, 3:6, :])
            for b in range(0, B, 2):
                for t in range(4):
                    for c in range(2):
                        ins = seq_pv(b + c, PTW[:, t, :], WV[:, b + c, t, :])
            ins.then_inc(win_used, 1)
            for g in range(NPG):
                key = ("st", g)
                banks.fill(pe, key, g % 4)
                for h in range(H):
                    if g == 0:
                        pe.wait_ge(ss_prob, h + 1)
                    ins = nc.tensor.transpose(BK[g % 4][:, P * h:P * h + P], S_SLC[:, h, P * g:P * g + P], ident)
                banks.filled(ins, key)
            banks.fill(pe, ("st", NPG), 4)
            for h in range(H):
                ins = nc.tensor.transpose(BK[4][0:32, P * h:P * h + P], S_SLC[:, h, PAST:PAST + 32], ident)
            banks.filled(ins, ("st", NPG))
            for g in range(NPG - 4, NPG + 1):
                banks.wait_given(pe, ("st", g))
            for b in range(0, B, 2):
                for c in range(2):
                    pe.wait_ge(vpage_loaded[(b + c) % 6], 256 * (b // 6 + 1))
                for g in range(NPG):
                    for c in range(2):
                        ins = seq_pv(b + c, PTS[:, 384 * g:384 * g + 384], VP[(b + c) % 6][:, g, :])
                ins.then_inc(kept, 1)
                for c in range(2):
                    ins = seq_pv(b + c, PTN[0:32, :], VN[0:32, 0:3, :], last=True)
                if b % 4 == 2:
                    banks.filled(ins, f"so{b // 4}")
            for q in range(2):
                banks.wait_given(pe, f"so{q}")
            for par in range(2):
                banks.fill(pe, ("sot", par), 4 + par)
                r = 64 * par
                for j in range(B // 2):
                    for h in range(H):
                        ins = nc.tensor.matmul(BK[4 + par][0:64, 64 * h + 16 * j:64 * h + 16 * j + 16],
                                               SO[r:r + 48, j, 64 * h:64 * h + 64], ident[r:r + 48, r + 16 * h:r + 16 * h + 16],
                                               start=True, stop=True)
                banks.filled(ins, ("sot", par))
            for c in range(3):
                banks.wait_given(pe, ("mo", 1, c))
                banks.wait_given(pe, ("po", c))
            for par in range(2):
                banks.wait_given(pe, ("sot", par))
            gemm("out", 1, M, KC, N_OUT_SLAB, KC, post=post(5))
            norm_chunk(5, 7)
            for m in range(KC):
                norm_chunk(6, m)
            channel_mixer(1)

        S5 = SP5[:, :].rearrange("p (n c) -> p n c", c=SC)
        DT, TH, RR, U1, T0, T1, T2, CRE, CIM, CARRY0, CARRY1, T3, T4 = (S5[:, j, :] for j in range(13))
        CARRY = S5[:, 9:11, :]
        CB = STAT[:, 0:2]
        BLEND = STAT[:, 2:18]
        NMAX, RSUM, RINV = STAT[:, 20:22], STAT[:, 24:26], STAT[:, 28:30]
        ZERO = STAT[:, 40:56].rearrange("p (r c) -> p r c", r=2)
        H0 = pr("h0").rearrange("p (r c b) -> p r c b", r=2, c=SC)
        MAGIC = 1.5 * 2.0 ** 23
        TWO_PI = 6.283185

        def at(ap, off, dims):
            return bass.AP(ap.tensor, ap.offset + off, [list(ap.ap[0])] + dims)

        def by_head(x):
            return x.rearrange("p (h b r) -> p b h r", h=H, b=B)

        def by_seq(x):
            return x.rearrange("p (b h r) -> p b h r", h=H, b=B)

        @block.scalar
        def _(act):
            A = nc.scalar.activation
            act.wait_ge(x_loaded, 16)

            def squares(norm, m):
                A(Hn[:, m, :], X[:, m, :], ACT.Square).then_inc(sq_done, 1)

            def root(norm):
                banks.wait_given(act, ("norm", norm))
                A(RST[:, :], RST[:, :], ACT.Sqrt).then_inc(rt_done, 1)

            def mem_evac(l):
                for s in range(N_MEM_SLAB):
                    for t in range(2):
                        key = ("memkv", l, s, t)
                        banks.take(act, key)
                        b = banks.uses[key][0]
                        banks.give(A(MKV[:, t, 256 * s:256 * s + 256], BK[b][:, 0:256], ACT.Copy), key)
                key = ("memkT", l)
                banks.take(act, key)
                banks.give(A(MKT, BK[banks.uses[key][0]][:, :].rearrange("p (c n) -> p c n", c=2), ACT.Copy), key)

            def in_evac(l, m, scaled):
                key = ("in", l, m)
                banks.take(act, key)
                banks.give(A(Z[:, m, :], BK[banks.uses[key][0]][:, 0:T], ACT.Copy, scale=0.125 if scaled else 1.0), key)

            def mem_attend(l):
                for hd in range(4):
                    b = hd % 2
                    act.wait_ge(nmax_done, 5 * l + hd + 1)
                    if hd >= 2:
                        banks.take(act, ("mt", l, hd - 2))
                    for t in range(2):
                        ins = A(MP[b][:, t, :], BK[b][:, 256 * t:256 * t + 256], ACT.Exp, bias=NMAX[:, t:t + 1],
                                accum_out=RSUM[:, t:t + 1])
                        if t == 1:
                            banks.give(ins, ("ms", l, hd))
                    if hd >= 1:
                        turned(l, hd - 1)
                turned(l, 3)
                act.wait_ge(nmax_done, 5 * l + 5)
                banks.give(A(MP[0][:, 0, :], BK[0][:, 0:256], ACT.Exp, bias=NMAX[:, 0:1], accum_out=RSUM[:, 0:1]),
                           ("ms", l, 4))
                key = ("mt", l, 4)
                banks.take(act, key)
                banks.give(A(MPT[:, 0:256], BK[2][:, 0:256], ACT.Copy), key)
                key = ("mo", l, 2)
                banks.take(act, key)
                for r in range(2):
                    o = BK[3][64 * r:64 * r + 64, 0:128].rearrange("p (c b g) -> p c b g", c=2, b=B)[:, :, :, 4 * r:4 * r + 4]
                    d = M[64 * r:64 * r + 64, 6:8, TP:T].rearrange("p c (b t) -> p c b t", b=B)
                    ins = A(d, o, ACT.Copy)
                    if r == 1:
                        banks.give(ins, key)

            def turned(l, hd):
                key = ("mt", l, hd)
                banks.take(act, key)
                banks.give(A(MPT, BK[2][:, :], ACT.Copy), key)
                if hd % 2 == 1:
                    key = ("mo", l, hd // 2)
                    banks.take(act, key)
                    banks.give(A(M[:, 6 + hd // 2, 0:TP], BK[3][:, 0:TP], ACT.Copy), key)

            def out_evac(name, l, norm, m):
                key = (name, l, m)
                b = banks.uses[key][0]
                banks.take(act, key)
                A(Hn[:, m, :], BK[b][:, 0:T], ACT.Square).then_inc(sq_done, 1)
                banks.give(A(Z[:, m, :], BK[b][:, 0:T], ACT.Copy), key)

            def channel_mixer(l):
                def silu(u, i=None):
                    key = ("fi", l, u if i is not None else "last", 0)
                    up = ("fi", l, u if i is not None else "last", 1)
                    banks.take(act, key, i)
                    banks.wait_former(act, up, i)
                    ins = A(Z[:, 8 + u % SLOTS, :], BK[2 * (u % SLOTS)][:, 0:T], ACT.Silu)
                    banks.give(ins, key)
                with act.Fori(0, FI // SLOTS) as i:
                    for u in range(SLOTS):
                        silu(u, i)
                silu(FI - 1)
                for m in range(KC):
                    out_evac("fo", l, 4 * l + 3, m)

            for m in range(KC):
                squares(0, m)
            act.wait_ge(memt_loaded, 16)
            act.dma_start(AR[:, 0:4096], memk_in[0]).then_inc(mkv_loaded, 16)
            act.dma_start(AR[:, 4096:8192], memv_in[0]).then_inc(mkv_loaded, 16)
            act.dma_start(U[:, 0:4096], w1s_in).then_inc(w1_loaded, 16)
            root(0)
            act.wait_ge(prm_loaded, 16)
            A(DT, pr("log_dt"), ACT.Exp).then_inc(dt_done[1], 1)
            mem_evac(0)
            act.wait_ge(dt_done[0], 1)
            A(RR, T0, ACT.Exp).then_inc(dt_done[1], 1)
            act.wait_ge(trig_arg, 1)
            A(SIN, SIN, ACT.Sin, scale=TWO_PI).then_inc(trig_done, 1)
            A(COS, COS, ACT.Sin, scale=-TWO_PI, bias=c1("halfpi")).then_inc(trig_done, 1)
            for m in range(8):
                in_evac(0, m, m >= 6)
            act.wait_ge(bt_cleared, 1)
            for r in range(2):
                for part in range(2):
                    key = ("bt", r, part)
                    banks.take(act, key)
                    nk = 4 if part == 0 else 2
                    for q in range(4):
                        dst = BT[r][32 * q:32 * q + 32, :, :].rearrange("p (k q) n -> p k q n", q=4)[:, 4 * part:4 * part + nk, q, :]
                        src = BK[banks.uses[key][0]][32 * q:32 * q + 32, 0:P * nk].rearrange("p (k n) -> p k n", n=P)
                        ins = A(dst, src, ACT.Copy)
                    banks.give(ins, key)
            mem_attend(0)

            def hidden(u, c, i):
                key = ("hc", u, c)
                banks.take(act, key, i)
                src = BK[5 + c][:, 0:387].rearrange("p (h n) -> p h n", n=129)[:, :, 1:1 + NCMP]
                banks.give(A(HCMP[c].rearrange("p (h n) -> p h n", h=H), src, ACT.Gelu_apprx_tanh, bias=CB[:, c:c + 1]), key)

            def keys_out(u, i):
                banks.take(act, ("ck", u), i)
                dst = KCT[64 * u:64 * u + 64, bass.ds(i, 1), :].rearrange("p a n -> p (a n)")
                banks.give(A(dst, BK[7][64 * u:64 * u + 64, 0:H * NCMP], ACT.Copy), ("ck", u))

            def values_out(u, i):
                banks.take(act, ("cv", u), i)
                dst = VC[0:NCMP, bass.ds(i * 2 + u, 1), :].rearrange("p a n -> p (a n)")
                banks.give(A(dst, BK[7][0:NCMP, 0:H * 64], ACT.Copy), ("cv", u))

            banks.wait_given(act, "pe")
            with act.Fori(0, 4) as i:
                for u in range(2):
                    hidden(u, 0, i)
                    if u == 1:
                        values_out(0, i)
                    hidden(u, 1, i)
                    keys_out(u, i)
                values_out(1, i)
            for k in range(6):
                banks.wait_given(act, f"u{k // 2}")
                A(Z[:, k, :], Z[:, k, :], ACT.Gelu_apprx_tanh).then_inc(glu_in, 1)
            for m in range(6):
                key = ("glu", 0, m)
                banks.take(act, key)
                banks.give(A(Hn[:, m, :], BK[banks.uses[key][0]][:, 0:T], ACT.Sigmoid, bias=pr("b_glu")[:, m:m + 1]), key)
            for m in range(KC):
                out_evac("out", 0, 1, m)
            root(1)
            for m in range(KC):
                act.wait_ge(x_done, m + 1)
                squares(2, m)
            root(2)
            channel_mixer(0)
            root(3)

            C = lambda out, in_: A(out, in_, ACT.Copy)
            mem_evac(1)
            for m in range(KC):
                act.wait_ge(x_done, KC + m + 1)
                squares(4, m)
            root(4)
            for m in range(17):
                in_evac(1, m, m < 6 or m >= 15)
            banks.take(act, "gates")
            b = banks.uses["gates"][0]
            A(GP, BK[b][:, 0:72].rearrange("p (t n) -> p t n", t=2), ACT.Sigmoid)
            banks.give(A(GS[0:32, :], BK[b][0:32, 72:108], ACT.Sigmoid), "gates")
            mem_attend(1)
            act.wait_ge(state_stored, 32)
            for c in range(2):
                banks.take(act, ("pc", c))
                banks.give(A(HCP[:, c, :], BK[5 + c][:, 0:H * NCP], ACT.Gelu_apprx_tanh, bias=CB[:, c:c + 1]), ("pc", c))
            for b3 in range(3):
                banks.take(act, ("vt", b3))
                src = BK[b3][:, :].rearrange("p (t j n) -> p t j n", t=2, j=2)[:, :, :, 64:128]
                banks.give(C(VT[:, :, 2 * b3:2 * b3 + 2, :], src), ("vt", b3))
            banks.take(act, "pck")
            banks.give(C(KCP, BK[3][:, 0:H * NCP]), "pck")
            banks.take(act, "pcv")
            banks.give(C(VCP[0:NCP, :], BK[4][0:NCP, 0:H * 64]), "pcv")
            act.wait_ge(cp_scored, 1)
            A(SCP, SCP, ACT.Exp).then_inc(cp_exp, 1)
            for n in range(6):
                banks.take(act, ("pct", n))
                banks.give(C(PTC[0:NCP, 2 * n:2 * n + 2, :].rearrange("p g q -> p (g q)"), BK[5 + n % 2][0:NCP, :]), ("pct", n))

            def scores_out(step):
                b, c, h = step // 12, step // 3 % 4, step % 3
                banks.take(act, ("sk", step))
                banks.give(C(S_SLC[32 * b:32 * b + 32, h, WIN * c:WIN * c + WIN], BK[7][32 * b:32 * b + 32, :]), ("sk", step))

            for n in range(14):
                if n < 12:
                    act.wait_ge(u_max, n + 1)
                    for gg in range(2):
                        for t in range(2):
                            s = SU[n % 2][:, gg, P * t:P * t + P * (t + 1)]
                            j = 2 * t + gg
                            ins = A(s, s, ACT.Exp, bias=NM[n % 2][:, j:j + 1], accum_out=RS[n % 2][:, j:j + 1])
                    ins.then_inc(u_exp, 1)
                if n >= 2:
                    scores_out(4 * (n - 2))
                if 1 <= n < 13:
                    for gg in range(2):
                        key = ("ut", n - 1, gg)
                        banks.take(act, key)
                        banks.give(C(PTU[(n - 1) % 2][:, gg, :], BK[4 + gg][:, 0:3 * P]), key)
                if n >= 2:
                    scores_out(4 * (n - 2) + 1)
                if n >= 2 and (n - 2) % 4 == 3:
                    h = (n - 2) // 4
                    banks.take(act, ("po", h))
                    banks.give(C(M[:, 2 * h:2 * h + 2, 0:TP], BK[6][:, :].rearrange("p (c n) -> p c n", c=2)), ("po", h))
                for j in range(2 if n >= 2 else 0):
                    scores_out(4 * (n - 2) + 2 + j)
            for j3 in range(2):
                banks.take(act, ("vn", j3))
                src = BK[4 + j3][0:32, 0:3 * P].rearrange("p (j n) -> p j n", j=3)[:, :, 64:128]
                banks.give(C(VN[0:32, 3 * j3:3 * j3 + 3, :], src), ("vn", j3))

            def row_exp(buf, j0, started, n, done):
                act.wait_ge(started, n)
                for h in range(H):
                    ins = A(buf(h), buf(h), ACT.Exp, bias=NS[:, j0 + h:j0 + h + 1], accum_out=SS[:, j0 + h:j0 + h + 1])
                ins.then_inc(done, 1)
            row_exp(lambda h: PC[:, h, 0:NCMP], 6, sc_max, 1, sc_exp)
            row_exp(lambda h: SW[:, h, :], 3, sw_max, 1, sw_exp)
            banks.take(act, "sct")
            banks.give(C(by_seq(PCT[0:NCMP, :]), by_head(BK[5][0:NCMP, 0:384])), "sct")
            for t in range(5):
                banks.take(act, ("swt", t))
                n, dst = (P, PTW[:, t, :]) if t < 4 else (32, PTN[0:32, :])
                ins = C(by_seq(dst), by_head(BK[t % 4][0:n, 0:384]))
                banks.give(ins, ("swt", t))
            act.wait_ge(win_used, 1)
            for h in range(H):
                act.wait_ge(ss_max, h + 1)
                A(S_SLC[:, h, :], S_SLC[:, h, :], ACT.Exp, bias=NS[:, h:h + 1], accum_out=SS[:, h:h + 1]).then_inc(ss_exp, 1)
            for g in range(0, NPG, 2):
                banks.take(act, ("st", g))
                banks.give(C(by_seq(PTS[:, 384 * g:384 * g + 384]), by_head(BK[g % 4][:, 0:384])), ("st", g))
            banks.take(act, ("st", NPG))
            banks.give(C(by_seq(PTN[0:32, :]), by_head(BK[4][0:32, 0:384])), ("st", NPG))
            act.wait_ge(kv_stored, 16)
            for m in range(KC):
                out_evac("out", 1, 5, m)
            root(5)
            for m in range(KC):
                act.wait_ge(x_done, 2 * KC + m + 1)
                squares(6, m)
            root(6)
            channel_mixer(1)
            root(7)

        @block.gpsimd
        def _(pool):
            tt = nc.gpsimd.tensor_tensor
            ch = Chain(pool, pool_seq)
            nc.gpsimd.memset(HID[:, 0:6144], 0.0).then_inc(bt_cleared, 1)

            def query_blocks(l, zq):
                ch.step(nc.gpsimd.memset(QMB, 0.0))
                for c in range(2):
                    banks.wait_given(pool, ("in", l, zq + c))
                for c in range(2):
                    for r in range(2):
                        dst = at(QMB[64 * r:64 * r + 64, c, :, :], 4 * r, [[72, B], [1, TS]])
                        src = Z[64 * r:64 * r + 64, zq + c, TP:T].rearrange("p (b t) -> p b t", b=B)
                        ins = nc.gpsimd.tensor_copy(dst, src)
                        if c + r == 2:
                            ins.then_inc(qmb_done, 1)
                            pool.wait_ge(qmb_done, l + 1)
                        else:
                            ch.step(ins)
            query_blocks(0, 6)
            ch.step(nc.gpsimd.memset(ZERO, 0.0))
            nc.gpsimd.memset(CARRY, 0.0).then_inc(carry0, 1)

            def states(o, width, cos, sin, sample, wait):
                pool.wait_ge(scanned, wait)
                w, hb = S5W[o % 2], S5H[o % 2]
                sh = (lambda x: x.rearrange("p (c b t) -> p c b t", c=OCT, b=B)) if sample else \
                     (lambda x: x.rearrange("p (c t) -> p c t", c=OCT))
                nn = OCT * width
                re, im = sh(w[:, 0:nn]), sh(w[:, 512:512 + nn])
                hr, hi = sh(hb[:, 0:nn]), sh(hb[:, 512:512 + nn])
                ta, tb = sh(S5G[:, 0:nn]), sh(S5G[:, 512:512 + nn])
                ch.tick(tt(hr, re, cos, ALU.mult))
                ch.tick(tt(hi, re, sin, ALU.mult))
                ch.tick(tt(ta, im, sin, ALU.mult))
                ch.tick(tt(tb, im, cos, ALU.mult))
                ch.sync()
                ch.tick(tt(hr, hr, ta, ALU.subtract))
                ch.tick(tt(hi, hi, tb, ALU.add))
                ch.sync()
                if sample:
                    for r in range(2):
                        src = sh(hb[:, 512 * r:512 * r + nn])[:, :, :, TS - 1]
                        ins = nc.gpsimd.tensor_copy(H0[:, r, OCT * o:OCT * o + OCT, :], src)
                else:
                    src = hb.rearrange("p (r c t) -> p r c t", r=2, c=OCT)[:, :, :, SEG - 1]
                    ins = tt(CARRY[:, :, OCT * o:OCT * o + OCT], src, ZERO, ALU.add)
                ins.then_inc(h5_done, 1)

            pool.wait_ge(trig_done, 2)
            with pool.Fori(0, NSEG) as i:
                ch.begin_loop(i, 6 * NO)
                for o in range(NO):
                    b, v, per, _ = banks.uses["y0"]
                    pool.wait_ge(banks.full[b], i * per + (v if o == 2 else v - 1))
                    states(o, SEG, COS[:, OCT * o:OCT * o + OCT, :], SIN[:, OCT * o:OCT * o + OCT, :], False,
                           i * NO + o + 1)
                ch.end_loop(NSEG)
            pool.wait_ge(h5_done, NO * NSEG)

            def few(x, o):
                return x[:, OCT * o:OCT * o + OCT, 0:TS].unsqueeze(2).to_broadcast([P, OCT, B, TS])
            banks.take(pool, "y2", NSEG - 1)
            for o in range(NO):
                if o == 2:
                    banks.take(pool, "u0")
                states(o, B * TS, few(COS, o), few(SIN, o), True, NO * NSEG + o + 1)

            banks.take(pool, ("hc", 1, 1), B // 2 - 1)
            query_blocks(1, 15)
            banks.wait_given(pool, ("mo", 1, 2))
            pool.wait_ge(memkv_stored, 32)
            for p in range(4):
                if p >= 2:
                    banks.take(pool, ("sk", 12 * p - 13))
                load_key_pages(pool, POOL, 2 * p + 1, p % 2)
            for b in range(1, B, 2):
                wait_value_slot(pool, b)
                load_value_pages(pool, POOL, b)

        @block.vector
        def _(dve):
            V = nc.vector
            ch = Chain(dve, dve_seq)
            tt, ts, stt = V.tensor_tensor, V.tensor_scalar, V.scalar_tensor_tensor

            def mean_square(norm):
                key = ("norm", norm)
                banks.take(dve, key)
                ch.sync()
                banks.give(ts(RST[:, :], BK[7][:, 0:T], 1.0 / D, EPS, ALU.mult, ALU.add), key)

            def pre_norm(norm):
                mean_square(norm)
                dve.wait_ge(rt_done, norm + 1)
                ch.step(V.reciprocal(RST[:, :], RST[:, :]))
                for k in range(KC):
                    stt(Hn[:, k, :], X[:, k, :], norm_g[:, norm, k:k + 1], RST[:, :], ALU.mult, ALU.mult)\
                        .then_inc(h_done, 1)

            def post_norm(norm):
                mean_square(norm)
                dve.wait_ge(rt_done, norm + 1)
                ch.step(V.reciprocal(RST[:, :], RST[:, :]))
                for k in range(KC):
                    ch.tick(stt(Z[:, k, :], Z[:, k, :], norm_g[:, norm, k:k + 1], RST[:, :], ALU.mult, ALU.mult))
                ch.sync()
                for k in range(KC):
                    tt(X[:, k, :], X[:, k, :], Z[:, k, :], ALU.add).then_inc(x_done, 1)

            def mem_soft(l):
                for hd in range(5):
                    key = ("ms", l, hd)
                    n = 2 if hd < 4 else 1
                    b = hd % 2
                    banks.take(dve, key)
                    if hd:
                        banks.wait_given(dve, ("ms", l, hd - 1))
                    V.tensor_reduce(NMAX[:, 0:n], BK[b][:, 0:256 * n].rearrange("p (t n) -> p t n", n=256), AX_X,
                                    ALU.max, negate=True).then_inc(nmax_done, 1)
                    banks.wait_given(dve, key)
                    ch.step(V.reciprocal(RINV[:, 0:n], RSUM[:, 0:n]))
                    for t in range(n):
                        ins = ts(MP[b][:, t, :], MP[b][:, t, :], RINV[:, t:t + 1], None, ALU.mult)
                        if t == n - 1:
                            ins.then_inc(prob_done, 1)

            def channel_mixer(l):
                def gate(u, i=None):
                    key = ("fi", l, u if i is not None else "last", 0)
                    up = ("fi", l, u if i is not None else "last", 1)
                    banks.wait_given(dve, key, i)
                    banks.take(dve, up, i)
                    dst = HD[:, FI - 1, :] if i is None else HD[:, bass.ds(i * SLOTS + u, 1), :].rearrange("p a n -> p (a n)")
                    banks.give(tt(dst, Z[:, 8 + u % SLOTS, :], BK[2 * (u % SLOTS) + 1][:, 0:T], ALU.mult), up)
                with dve.Fori(0, FI // SLOTS) as i:
                    for u in range(SLOTS):
                        gate(u, i)
                gate(FI - 1)

            dve.wait_ge(x_loaded, 16)
            dve.wait_ge(prm_loaded, 16)
            pre_norm(0)
            dve.wait_ge(dt_done[1], 1)
            tt(T0, pr("a_re"), DT, ALU.mult).then_inc(dt_done[0], 1)
            ch.step(tt(TH, pr("a_im"), DT, ALU.mult))
            ch.step(ts(U1, TH, 1.0 / (2 * np.pi), None, ALU.mult))
            ch.step(ts(T1, U1, MAGIC, MAGIC, ALU.add, ALU.subtract))
            ch.step(tt(U1, U1, T1, ALU.subtract))
            shape = [P, SC, SEG]
            dve.wait_ge(cst_loaded, 16)
            ch.step(tt(SIN, U1.unsqueeze(2).to_broadcast(shape), c1("tau").unsqueeze(1).to_broadcast(shape), ALU.mult))
            ch.step(ts(COS, SIN, MAGIC, MAGIC, ALU.add, ALU.subtract))
            ch.step(tt(SIN, SIN, COS, ALU.subtract))
            stt(COS, SIN, 0.25, SIN, ALU.is_gt, ALU.subtract).then_inc(trig_arg, 1)
            dve.wait_ge(dt_done[1], 2)
            r0 = R0.rearrange("p (c t) -> p c t", t=SEG)
            r0s = R0S.rearrange("p (c b t) -> p c b t", c=SC, b=B)
            ch.tick(V.tensor_copy(r0, RR.unsqueeze(2).to_broadcast(shape)))
            ch.tick(V.tensor_copy(r0s, RR.unsqueeze(2).unsqueeze(3).to_broadcast([P, SC, B, TS])))
            ch.sync()
            ch.tick(V.memset(r0[:, :, 0], 0.0))
            ch.tick(V.memset(r0s[:, :, :, 0], 0.0))
            for r in range(2):
                ch.tick(tt(H0[:, r, :, :], H0[:, r, :, :], RR.unsqueeze(2).to_broadcast([P, SC, B]), ALU.mult))
            dve.wait_ge(trig_done, 2)
            ch.tick(tt(T1, RR, COS[:, :, 0], ALU.mult))
            ch.tick(tt(T2, RR, SIN[:, :, 0], ALU.mult))
            ch.tick(tt(T3, pr("a_re"), pr("a_re"), ALU.mult))
            ch.tick(tt(T4, pr("a_im"), pr("a_im"), ALU.mult))
            ch.sync()
            ch.tick(ts(T1, T1, -1.0, None, ALU.add))
            ch.step(tt(T3, T3, T4, ALU.add))
            ch.tick(V.reciprocal(T3, T3))
            ch.tick(tt(CRE, T1, pr("a_re"), ALU.mult))
            ch.tick(tt(T4, T2, pr("a_im"), ALU.mult))
            ch.sync()
            ch.step(tt(CRE, CRE, T4, ALU.add))
            ch.tick(tt(CRE, CRE, T3, ALU.mult))
            ch.tick(tt(CIM, T2, pr("a_re"), ALU.mult))
            ch.tick(tt(T4, T1, pr("a_im"), ALU.mult))
            ch.sync()
            ch.step(tt(CIM, CIM, T4, ALU.subtract))
            ch.step(tt(CIM, CIM, T3, ALU.mult))
            dve.wait_ge(smat_loaded, 32)
            big = [P, SC, 32]
            cre, cim = (x.unsqueeze(2).to_broadcast(big) for x in (CRE, CIM))
            ch.tick(tt(BX[0], BIN[0], cre, ALU.mult))
            ch.tick(tt(BX[2], BIN[1], cim, ALU.mult))
            ch.sync()
            tt(BX[0], BX[0], BX[2], ALU.subtract).then_inc(bx_done, 1)
            ch.tick(tt(BX[1], BIN[0], cim, ALU.mult))
            dve.wait_ge(bx_done, 1)
            ch.tick(tt(BX[2], BIN[1], cre, ALU.mult))
            ch.sync()
            tt(BX[1], BX[1], BX[2], ALU.add).then_inc(bx_done, 1)
            banks.take(dve, "pe")
            banks.give(tt(CB, BK[6][:, 0:2], pr("b1"), ALU.add), "pe")
            mem_soft(0)
            dve.wait_ge(carry0, 1)
            ch.step(ts(CM[1], CM[1], -1.0, None, ALU.mult))

            def scan_unit(o, key, width, cos, sin, sample, i, before):
                w = S5W[o % 2]
                sh = (lambda x: x.rearrange("p (c b t) -> p c b t", c=OCT, b=B)) if sample else \
                     (lambda x: x.rearrange("p (c t) -> p c t", c=OCT))
                nn = OCT * width
                wr, wi = sh(w[:, 0:nn]), sh(w[:, 512:512 + nn])
                ta = sh(S5T[:, 0:nn])
                re, im = sh(BK[0][:, 0:nn]), sh(BK[1][:, 0:nn])
                if before is not None:
                    dve.wait_ge(h5_done, before)
                ch.sync()
                banks.take(dve, key + "re", i)
                ch.tick(tt(wr, re, cos, ALU.mult))
                banks.take(dve, key + "im", i)
                ch.step(tt(ta, im, sin, ALU.mult))
                ch.tick(tt(wr, wr, ta, ALU.add))
                banks.give(tt(wi, im, cos, ALU.mult), key + "im")
                ch.sync()
                banks.give(tt(ta, re, sin, ALU.mult), key + "re")
                banks.wait_given(dve, key + "im", i)
                banks.wait_given(dve, key + "re", i)
                ch.tick(tt(wi, wi, ta, ALU.subtract))
                if sample:
                    ch.sync()
                    for r in range(2):
                        x = sh(w[:, 512 * r:512 * r + nn])[:, :, :, 0]
                        ch.tick(tt(x, x, H0[:, r, OCT * o:OCT * o + OCT, :], ALU.add))
                else:
                    bl = BLEND.rearrange("p (r c) -> p r c", r=2)
                    ch.tick(tt(bl, CARRY[:, :, OCT * o:OCT * o + OCT],
                               RR[:, OCT * o:OCT * o + OCT].unsqueeze(1).to_broadcast([P, 2, OCT]), ALU.mult))
                    ch.sync()
                    x = w.rearrange("p (r c t) -> p r c t", r=2, c=OCT)[:, :, :, 0]
                    ch.tick(tt(x, x, bl, ALU.add))
                ch.sync()
                d0 = (R0S if sample else R0)[:, nn * o:nn * o + nn]
                ch.tick(V.tensor_tensor_scan(w[:, 0:nn], d0, w[:, 0:nn], 0.0, ALU.mult, ALU.add))
                V.tensor_tensor_scan(w[:, 512:512 + nn], d0, w[:, 512:512 + nn], 0.0, ALU.mult, ALU.add).then_inc(scanned, 1)

            def y_unit(o, key, width, i):
                banks.take(dve, key, i)
                for ku in range(2):
                    k = 2 * o + ku
                    z = Z[:, k, TP:T] if i is None else Z[:, k, bass.ds(i * SEG, SEG)]
                    ins = stt(z, z, pr("d")[:, k:k + 1], BK[4][:, ku * width:ku * width + width], ALU.mult, ALU.add)
                    if ku == 0:
                        ch.tick(ins)
                    else:
                        banks.give(ins, key)

            with dve.Fori(0, NSEG) as i:
                ch.begin_loop(i, NO * 8)
                for o in range(NO):
                    scan_unit(o, f"s5{o}", SEG, COS[:, OCT * o:OCT * o + OCT, :], SIN[:, OCT * o:OCT * o + OCT, :],
                              False, i, (i * NO + o - 1) if o == 2 else i * NO)
                    if o:
                        y_unit(o - 1, f"y{o - 1}", SEG, i)
                y_unit(2, "y2", SEG, i)
                ch.end_loop(NSEG)

            def few(x, o):
                return x[:, OCT * o:OCT * o + OCT, 0:TS].unsqueeze(2).to_broadcast([P, OCT, B, TS])
            for o in range(NO):
                scan_unit(o, f"t5{o}", B * TS, few(COS, o), few(SIN, o), True, None, NO * NSEG + (o - 1 if o == 2 else 0))
                if o:
                    y_unit(o - 1, f"u{o - 1}", B * TS, None)
            y_unit(NO - 1, f"u{NO - 1}", B * TS, None)
            for m in range(6):
                banks.wait_given(dve, ("glu", 0, m))
                tt(M[:, m, :], Hn[:, m, :], Z[:, m, :], ALU.mult).then_inc(mix_done, 1)
            post_norm(1)
            pre_norm(2)
            channel_mixer(0)
            post_norm(3)

            pre_norm(4)
            mem_soft(1)
            dve.wait_ge(cst2_loaded, 16)
            banks.take(dve, "rowgates")
            banks.give(tt(GT, BK[4][:, 0:36].rearrange("p (n g) -> p n g", g=G),
                          c2("gsel").unsqueeze(1).to_broadcast([P, 9, G]), ALU.mult), "rowgates")
            banks.wait_given(dve, "rowgates")
            ch.tick(V.tensor_reduce(GR, GT, AX_X, ALU.add))
            for m in range(9, 15):
                banks.wait_given(dve, ("in", 1, m))
            V.tensor_copy(KD[64:128, :, :], Z[0:64, 9:15, 0:TP]).then_inc(kd_done, 1)
            ch.step(V.memset(QBD, 0.0))
            for g in range(G):
                src = Z[64 * (g % 2):64 * (g % 2) + 64, g // 2:6:2, TP:T]
                for c in range(2):
                    dst = QBD[64 * c:64 * c + 64, :, :, 16 * c + 4 * g:16 * c + 4 * g + 4]
                    ins = V.tensor_copy(dst, src.rearrange("p h (b c t) -> p b h c t", b=4, c=2)[:, :, :, c, :])
                    if g * 2 + c < 7:
                        ch.step(ins)
            ins.then_inc(qbd_done, 1)
            dve.wait_ge(state_stored, 32)
            slopes = [float(np.exp2(-8.0 * (n + 1) / 12)) for n in range(12)]
            cd = c2("cmask_d").rearrange("p (t n) -> p t n", t=2)
            cm = c2("cmask_m").rearrange("p (t n) -> p t n", t=2)
            for par in range(2):
                key = ("pcs", par)
                banks.take(dve, key)
                v = BK[5 + par][:, 0:12 * NCP].rearrange("p (t h g n) -> p t h g n", t=2, h=H, g=2)
                for h in range(H):
                    for gg in range(2):
                        hd = 4 * h + par + 2 * gg
                        ins = stt(SCP[:, :, hd, :], cd, slopes[hd], v[:, :, h, gg, :], ALU.mult, ALU.add)
                        if h * 2 + gg < 5:
                            ch.tick(ins)
                        else:
                            banks.give(ins, key)
            ch.sync()
            banks.wait_given(dve, ("pcs", 0))
            banks.wait_given(dve, ("pcs", 1))
            scp = SCP.rearrange("p t g n -> p (t g) n")
            full = [P, 24, NCP]
            ch.step(V.tensor_reduce(CMX, scp, AX_X, ALU.max, negate=True))
            tt(scp, scp, CMX.unsqueeze(2).to_broadcast(full), ALU.add).then_inc(cp_scored, 1)
            dve.wait_ge(cp_exp, 1)
            ch.step(tt(SCP, SCP, cm.unsqueeze(2).to_broadcast([P, 2, 12, NCP]), ALU.mult))
            ch.step(V.tensor_reduce(CSM, scp, AX_X, ALU.add))
            ch.step(ts(CSM, CSM, 1e-30, None, ALU.max))
            ch.step(V.reciprocal(CSM, CSM))
            banks.wait_given(dve, "gates")
            ch.step(tt(CSM.rearrange("p (t g) -> p t g", t=2), CSM.rearrange("p (t g) -> p t g", t=2), GP[:, :, 0:12], ALU.mult))
            tt(scp, scp, CSM.unsqueeze(2).to_broadcast(full), ALU.mult).then_inc(cp_prob, 1)

            def unit_max(n):
                h, par = n // 4, n // 2 % 2
                s = SU[n % 2]
                if n >= 2:
                    for gg in range(2):
                        banks.take(dve, ("ut", n - 2, gg))
                for gg in range(2):
                    banks.take(dve, ("us", n, gg))
                    banks.give(stt(s[:, gg, :], c2("causal"), slopes[4 * h + par + 2 * gg], BK[2 * (n % 2) + gg][:, 0:3 * P],
                                   ALU.mult, ALU.add), ("us", n, gg))
                for gg in range(2):
                    banks.wait_given(dve, ("us", n, gg))
                ch.step(V.tensor_reduce(NM[n % 2][:, 0:2], s[:, :, 0:P], AX_X, ALU.max, negate=True))
                V.tensor_reduce(NM[n % 2][:, 2:4], s[:, :, P:3 * P], AX_X, ALU.max, negate=True).then_inc(u_max, 1)

            def unit_prob(n):
                h, par, br = n // 4, n // 2 % 2, n % 2
                dve.wait_ge(u_exp, n + 1)
                if n:
                    dve.wait_ge(u_prob, n)
                ch.step(V.reciprocal(RW, RS[n % 2]))
                o = (1 + br) * 12 + 4 * h + par
                rw = RW.rearrange("p (t g) -> p t g", t=2)
                ch.step(tt(rw, rw, GP[:, :, o:o + 3:2], ALU.mult))
                for gg in range(2):
                    for t in range(2):
                        s = SU[n % 2][:, gg, P * t:P * t + P * (t + 1)]
                        ins = ts(s, s, RW[:, 2 * t + gg:2 * t + gg + 1], None, ALU.mult)
                        if gg + t < 2:
                            ch.tick(ins)
                ins.then_inc(u_prob, 1)

            for n in range(13):
                if n < 12:
                    unit_max(n)
                if n >= 1:
                    unit_prob(n - 1)

            banks.take(dve, ("po", 2))
            for g in range(G):
                src = Z[64 * (g % 2):64 * (g % 2) + 64, g // 2:6:2, TP:T]
                dst = Q0[0:64, :, :].rearrange("p h (b g t) -> p h b g t", b=B, g=G)[:, :, :, g, :]
                ins = V.tensor_copy(dst, src.rearrange("p h (b t) -> p h b t", b=B))
                if g < 3:
                    ch.step(ins)
            ins.then_inc(q_done, 1)
            slope = c2("slope")
            banks.take(dve, "snew")
            for j in range(6):
                dst = SNEW[:, j, :] if j < 3 else SW[:, j - 3, WIN:WIN + 32]
                ins = stt(dst, c2("new_d"), slope[:, j % 3:j % 3 + 1], BK[0][:, 32 * j:32 * j + 32], ALU.mult, ALU.add)
                if j < 5:
                    ch.tick(ins)
                else:
                    banks.give(ins, "snew")
            banks.take(dve, "scs")
            ch.tick(V.memset(PC[:, :, NCMP], 0.0))
            for h in range(H):
                ins = stt(PC[:, h, 0:NCMP], c2("cmp_d"), slope[:, h:h + 1], BK[1][:, P * h:P * h + NCMP], ALU.mult, ALU.add)
                if h < 2:
                    ch.tick(ins)
                else:
                    banks.give(ins, "scs")
            banks.wait_given(dve, "scs")
            V.tensor_reduce(NS[:, 6:9], PC[:, :, 0:NCMP], AX_X, ALU.max, negate=True).then_inc(sc_max, 1)
            for h in range(H):
                banks.take(dve, ("sws", h))
                banks.give(stt(SW[:, h, 0:WIN], c2("win_d"), slope[:, h:h + 1], BK[(2, 3, 4)[h]][:, :], ALU.mult, ALU.add), ("sws", h))
            for h in range(H):
                banks.wait_given(dve, ("sws", h))
            banks.wait_given(dve, "snew")
            V.tensor_reduce(NS[:, 3:6], SW, AX_X, ALU.max, negate=True).then_inc(sw_max, 1)
            dve.wait_ge(sc_exp, 1)
            ch.step(V.reciprocal(SS[:, 6:9], SS[:, 6:9]))
            for h in range(H):
                ch.tick(ts(PC[:, h, 0:NCMP], PC[:, h, 0:NCMP], SS[:, 6 + h:7 + h], None, ALU.mult))
            ch.sync()
            pc4 = PC.rearrange("p h (j n) -> p h j n", n=4)
            ch.step(V.tensor_reduce(IMP[:, :, 0:NBLK], pc4, AX_X, ALU.add))
            tt(IMP[:, :, 1:NBLK], IMP[:, :, 1:NBLK], pc4[:, :, 0:NBLK - 1, 3], ALU.add).then_inc(imp_done, 1)
            dve.wait_ge(imp_done, 1)
            for h in range(H):
                ins = ts(PC[:, h, 0:NCMP], PC[:, h, 0:NCMP], GR[:, h:h + 1], None, ALU.mult)
                if h < 2:
                    ch.tick(ins)
            ins.then_inc(sc_prob, 1)
            dve.wait_ge(sw_exp, 1)
            ch.step(V.reciprocal(SS[:, 3:6], SS[:, 3:6]))
            ch.step(tt(SS[:, 3:6], SS[:, 3:6], GR[:, 6:9], ALU.mult))
            for h in range(H):
                ins = ts(SW[:, h, :], SW[:, h, :], SS[:, 3 + h:4 + h], None, ALU.mult)
                if h < 2:
                    ch.tick(ins)
            ins.then_inc(sw_prob, 1)
            banks.take(dve, "imp")
            banks.give(V.tensor_copy(IMP[:, :, 0:NBLK], BK[5][:, 0:H * NBLK].rearrange("p (h j) -> p h j", h=H)), "imp")
            banks.wait_given(dve, "imp")
            ch.tick(V.memset(IMP[:, :, 0:1], -NEG))
            ch.tick(V.memset(IMP[:, :, NBLK - 1:NBLK + 1], -NEG))
            ch.sync()
            for h in range(H):
                for _ in range(2):
                    ch.step(V.max(TOP, IMP[:, h, :]))
                    ch.step(V.match_replace(IMP[:, h, :], TOP, IMP[:, h, :], TAKEN))
            ch.step(ts(MS, IMP, 0.5 * TAKEN, NEG, ALU.is_gt, ALU.mult))
            banks.wait_given(dve, ("sk", 47))
            dve.wait_ge(slcd_loaded, 16)
            ch.step(V.tensor_reduce(NEWMAX, SNEW, AX_X, ALU.max))
            for n in range(H + 1):
                if n < H:
                    s = S_SLC[:, n, :]
                    ch.tick(stt(s[:, 0:PAST], SLCD, slope[:, n:n + 1], s[:, 0:PAST], ALU.mult, ALU.add))
                    ch.tick(V.tensor_copy(s[:, PAST:PAST + 32], SNEW[:, n, :]))
                    ch.sync()
                    blk = s[:, 0:PAST].rearrange("p (j i) -> p j i", i=64)
                    mask = MS[:, n, 0:NBLK].unsqueeze(2).to_broadcast([P, NBLK, 64])
                    ch.step(V.tensor_tensor_reduce(blk, blk, mask, 1.0, NEWMAX[:, n:n + 1], ALU.add, ALU.max, NS[:, n:n + 1]))
                    ts(NS[:, n:n + 1], NS[:, n:n + 1], -1.0, None, ALU.mult).then_inc(ss_max, 1)
                if n:
                    dve.wait_ge(ss_exp, n)
                    ch.step(V.reciprocal(SS[:, n - 1:n], SS[:, n - 1:n]))
                    ch.step(tt(SS[:, n - 1:n], SS[:, n - 1:n], GR[:, 2 + n:3 + n], ALU.mult))
                    s = S_SLC[:, n - 1, :]
                    ts(s, s, SS[:, n - 1:n], None, ALU.mult).then_inc(ss_prob, 1)
            for g in range(1, NPG, 2):
                banks.take(dve, ("st", g))
                banks.give(V.tensor_copy(by_seq(PTS[:, 384 * g:384 * g + 384]), by_head(BK[g % 4][:, 0:384])), ("st", g))
            for q in range(2):
                banks.take(dve, f"so{q}")
                for r in (0, 64):
                    ins = V.tensor_copy(SO[r:r + 48, 2 * q:2 * q + 2, :].rearrange("p c n -> p (c n)"), BK[6 + q][r:r + 48, 0:384])
                    if r:
                        banks.give(ins, f"so{q}")
                    else:
                        ch.tick(ins)
            for par in range(2):
                banks.take(dve, ("sot", par))
                for g in range(G):
                    src = BK[4 + par][0:64, 0:192].rearrange("p (h j g t) -> p h j g t", h=H, j=B // 2, g=G)[:, :, :, g, :]
                    dst = M[64 * (g % 2):64 * (g % 2) + 64, g // 2:6:2, TP:T]
                    dst = dst.rearrange("p h (j c t) -> p h j c t", c=2, t=TS)[:, :, :, par, :]
                    ins = V.tensor_copy(dst, src)
                    if g < 3:
                        ch.tick(ins)
                    else:
                        banks.give(ins, ("sot", par))
            post_norm(5)
            pre_norm(6)
            channel_mixer(1)
            post_norm(7)

        @block.sync
        def _(sp):
            sources = {}
            for l in range(2):
                base8 = 0 if l == 0 else 10
                for s in range(N_MEM_SLAB):
                    sources[FIRST["mem", l] + s] = (w8_in[base8 + s], SLAB)
                for s in range(N_IN_SLAB if l == 0 else N_NSA_SLAB):
                    sources[FIRST["in", l] + s] = (w8_in[base8 + 2 + s], SLAB)
                for s in range(N_OUT_SLAB):
                    sources[FIRST["out", l] + s] = (w8_in[(6 if l == 0 else 21) + s], SLAB)
                for s in range(FI):
                    sources[FIRST["fi", l] + s] = (wfi_in[l, s], SLAB)
                for s in range(FO):
                    sources[FIRST["fo", l] + s] = (wfo_in[l, s], 11 * P)
            for s in range(N_GLU_SLAB):
                sources[FIRST["glu", 0] + s] = (wglu_in[s], 6 * 256)

            def wait_release(n):
                for l in range(2):
                    first = FIRST["fi", l]
                    if first <= n < first + FI // SLOTS * SLOTS:
                        s, v, per = released[first + (n - first) % SLOTS]
                        sp.wait_ge(s, v + per * ((n - first) // SLOTS))
                        return
                s, v, _ = released[n]
                sp.wait_ge(s, v)

            def load(n):
                if n >= SLOTS:
                    wait_release(n - SLOTS)
                src, w = sources[n]
                sp.dma_start(W[:, n % SLOTS, 0:w], src).then_inc(slab_loaded[n % SLOTS], 16)

            def load_stage(name, l, count):
                for s in range(count):
                    load(FIRST[name, l] + s)

            def load_mixer_in(l):
                first = FIRST["fi", l]
                for u in range(SLOTS):
                    load(first + u)
                with sp.Fori(0, FI // SLOTS - 1) as i:
                    for u in range(SLOTS):
                        s, v, per = released[first + u]
                        sp.wait_ge(s, i * per + v)
                        src = wfi_in[l, bass.ds(i * SLOTS + (SLOTS + u), 1), :, :].rearrange("a p n -> p (a n)")
                        sp.dma_start(W[:, (first + u) % SLOTS, :], src).then_inc(slab_loaded[(first + u) % SLOTS], 16)
                for n in range(first + FI // SLOTS * SLOTS, first + FI):
                    load(n)

            sp.dma_start(CS[:, :], cst1_in).then_inc(cst_loaded, 16)
            sp.dma_start(X_[:, :], x_in).then_inc(x_loaded, 16)
            sp.dma_start(PRM[:, :], prm_in).then_inc(prm_loaded, 16)
            sp.dma_start(M_[:, 0:KC * NMEM], mem_in).then_inc(memt_loaded, 16)
            load_stage("mem", 0, N_MEM_SLAB)
            sp.dma_start(XT[:, 0:1536], bmat_in).then_inc(smat_loaded, 16)
            sp.dma_start(U[:, 7168:8704], cmat_in).then_inc(smat_loaded, 16)
            sp.dma_start(PT[:, :], pages_in).then_inc(pt_loaded, 16)
            load_stage("in", 0, N_IN_SLAB)
            load_stage("glu", 0, N_GLU_SLAB)

            def store_mem_kv(l):
                for s in range(N_MEM_SLAB):
                    for t in range(2):
                        banks.wait_given(sp, ("memkv", l, s, t))
                sp.dma_start(memkv_out[l], AR[:, 8192:9216]).then_inc(memkv_stored, 16)
            store_mem_kv(0)
            banks.wait_given(sp, ("mo", 0, 2))
            sp.wait_ge(memkv_stored, 16)
            sp.wait_ge(pt_loaded, 16)

            def load_pages(b, s):
                with sp.Fori(0, NPG // PG_STEP) as i:
                    for u, r in enumerate(page_numbers(sp, SP, b, i, cmp_in)):
                        dst = AR[:, bass.ds(i * (384 * PG_STEP) + (6144 * s + 384 * u), 384)]
                        sp.dma_start(dst, page(cmp_in, r)).then_inc(page_loaded[s], 16)
            for b in range(B):
                if b >= 2:
                    banks.take(sp, ("hc", b % 2, 1), b // 2 - 1)
                load_pages(b, b % 2)
            load_stage("out", 0, N_OUT_SLAB)
            sp.dma_start(winold_out, winold_in).then_inc(stored, 16)
            banks.take(sp, ("hc", 0, 1), B // 2 - 1)
            banks.take(sp, ("hc", 1, 1), B // 2 - 1)
            sp.dma_start(AR[:, 0:4096], memk_in[1]).then_inc(mkv_loaded, 16)
            sp.dma_start(AR[:, 4096:8192], memv_in[1]).then_inc(mkv_loaded, 16)
            sp.wait_ge(h5_done, NO * NSEG + NO)
            sp.dma_start(st_p_out, CARRY).then_inc(state_stored, 16)
            sp.dma_start(st_s_out, pr("h0")).then_inc(state_stored, 16)
            load_mixer_in(0)
            sp.wait_ge(x_done, KC)
            sp.dma_start(M_[:, 0:KC * NMEM], mem_in).then_inc(memt_loaded, 16)
            sp.dma_start(XT[:, 0:C2N], cst2_in).then_inc(cst2_loaded, 16)
            sp.dma_start(U[:, 0:4096], w1p_in).then_inc(w1p_loaded, 16)
            sp.dma_start(SLCD, slcd_in).then_inc(slcd_loaded, 16)
            load_stage("fo", 0, FO)
            load_stage("mem", 1, N_MEM_SLAB)
            load_stage("in", 1, N_NSA_SLAB)
            for s in range(SLOTS):
                load(FIRST["out", 1] + s)
            for m in range(6, 15):
                banks.wait_given(sp, ("in", 1, m))
            sp.dma_start(kv_out, Z_[:, 6 * T:15 * T]).then_inc(kv_stored, 16)
            store_mem_kv(1)
            banks.wait_given(sp, ("mo", 1, 2))
            sp.wait_ge(memkv_stored, 32)
            for p in range(4):
                if p >= 2:
                    banks.take(sp, ("sk", 12 * p - 13))
                load_key_pages(sp, SP, 2 * p, p % 2)
            banks.take(sp, ("sk", 35))
            for b in range(4):
                sp.dma_start(AR[:, 1536 * b:1536 * b + 1536], wink_in[b]).then_inc(win_loaded, 16)
            banks.take(sp, ("sk", 47))
            sp.dma_start(AR[:, 6144:12288], winv_in).then_inc(win_loaded, 16)
            for b in range(0, B, 2):
                wait_value_slot(sp, b)
                load_value_pages(sp, SP, b)
            load(FIRST["out", 1] + 3)
            load_mixer_in(1)
            load_stage("fo", 1, FO)
            sp.wait_ge(x_done, 4 * KC)
            sp.dma_start(y_out, X_[:, :]).then_inc(stored, 16)
            sp.wait_ge(stored, 32)
            sp.wait_ge(state_stored, 32)
            sp.wait_ge(kv_stored, 16)
    return nc


_OUTS = [("y", (P, KC * T)), ("state_prompt", (P, 2, SC)), ("state_sample", (P, 2 * SC * B)),
         ("kv", (P, 9 * T)), ("win_old", (B, WIN - TS, H * 128)), ("mem_kv", (2, P, 2 * 512))]


def _constants():
    f = np.float32
    c1 = np.zeros((P, C1N), f)
    c1[:, slice(*C1["ident"])] = np.eye(P)
    c1[:, slice(*C1["ones"])] = 1
    c1[:, slice(*C1["tau"])] = np.arange(1, SEG + 1)
    c1[:, C1["halfpi"][0]] = np.pi / 2
    c1[:, C1["eps"][0]] = EPS
    c2 = np.zeros((P, C2N), f)
    q = np.arange(P)[:, None]

    def put(name, v):
        c2[:, slice(*C2[name])] = np.broadcast_to(v, (P, C2[name][1] - C2[name][0]))
    k = np.arange(256)[None, :]
    d0 = np.where(k[:, :P] <= q, k[:, :P] - q, NEG)
    d1 = np.where(k <= P + q, k - P - q, NEG)
    put("causal", np.concatenate([d0, d1], 1))
    e = 16 * np.arange(NCP)[None, :] + 31
    dist = np.concatenate([q - e, q + P - e], 1)
    put("cmask_d", np.where(dist >= 0, -dist, NEG))
    put("cmask_m", dist >= 0)
    g, t = (q // 4) % 4, q % 4
    put("cmp_d", 16 * np.arange(NCMP)[None, :] + 31 - PAST - t)
    w = np.arange(WIN)[None, :]
    put("win_d", np.where(w > t, w - WIN - t, NEG))
    bt = np.arange(32)[None, :]
    put("new_d", np.where((bt // 4 == q // 16) & (bt % 4 <= t), bt % 4 - t, NEG))
    slopes = np.exp2(-8.0 * (np.arange(12) + 1.0) / 12).reshape(H, G)
    put("slope", slopes[:, g[:, 0]].T)
    put("gsel", g == np.arange(4)[None, :])
    put("same", (q // 16 == q.T // 16) & (q % 4 == q.T % 4))
    j = np.arange(33)
    put("earlier", (j[None, :] < j[:, None]).reshape(1, -1))
    sp = np.zeros((P, P), f)
    r = np.arange(P)
    sp[(r // 16) * 4 + r % 4, r] = 1
    put("spread", sp)
    slcd = (np.arange(PAST)[None, :] - PAST - t).astype(f)
    return c1, c2, slcd


def kernel(**inputs):
    import concourse.bacc as _bacc
    from concourse.bass_utils import run_bass_kernel_spmd as _run

    a = {k: np.asarray(v) for k, v in inputs.items()}

    def feature_major(x):
        return x.T.reshape(-1, P, x.shape[0]).transpose(1, 0, 2).reshape(P, -1)

    def slabs(w):
        k, n = w.shape
        return w.reshape(k // P, P, n // 256, 256).transpose(2, 1, 0, 3).reshape(n // 256, P, -1)

    def states(x):
        return x.reshape((SC, P) + x.shape[2:]).swapaxes(0, 1)

    c1, c2, slcd = _constants()
    x = feature_major(np.concatenate([a["x_prompt"][0], a["x_sample"].reshape(B * TS, D)]))
    w8 = []
    for l in range(2):
        wm = a["w_mem_kv"][l].reshape(D, 2, 2, 2, 64).transpose(0, 1, 3, 2, 4).reshape(D, 512)
        w8.append(slabs(wm))
        if l == 0:
            w8.append(slabs(a["ssm_w_in"][0]))
        else:
            w = a["nsa_w_in"][0]
            w8.append(slabs(np.concatenate([w[:, :1920], w[:, 1956:2212], w[:, 1920:1956], np.zeros((D, 92), w.dtype)], 1)))
        w8.append(slabs(a["w_out"][l]))
    w8 = np.concatenate(w8)
    wfi = a["w_ffn_in"].reshape(2, KC, P, 2, FC, P).transpose(0, 4, 2, 1, 3, 5).reshape(2, FC, P, SLAB)
    wfo = a["w_ffn_out"].reshape(2, 2, 11, P, KC, P).transpose(0, 4, 1, 3, 2, 5).reshape(2, FO, P, 11 * P)
    w1 = a["nsa_cmp_w1"][0].reshape(2, 16, 2, 64, P)
    w1s = w1.reshape(2, 8, 2, 2, 64, P).transpose(2, 4, 3, 0, 1, 5).reshape(P, -1)
    w1p = w1.transpose(2, 3, 0, 1, 4).reshape(P, -1)
    pe = a["nsa_cmp_pe"][0].reshape(2, 8, 2, 2, 64).transpose(2, 4, 3, 0, 1).reshape(P, 32)
    prm = np.zeros((P, PRN), np.float32)
    norms = np.stack([a[n][l] for l in range(2) for n in ("norm_mix_pre", "norm_mix_post", "norm_ffn_pre", "norm_ffn_post")])
    dt = np.repeat(a["ssm_log_dt"][0][:, None], 64, 1)
    h0 = np.stack([states(a[n][0].transpose(1, 2, 0)) for n in ("state_ssm_re", "state_ssm_im")], 1)
    for name, v in (("norm", norms.reshape(8, KC, P).transpose(2, 0, 1)), ("a_re", states(a["ssm_a_re"][0])),
                    ("a_im", states(a["ssm_a_im"][0])), ("log_dt", states(dt)), ("h0", h0),
                    ("d", a["ssm_d"][0].reshape(6, P).T), ("b_glu", a["ssm_b_glu"][0].reshape(6, P).T),
                    ("w2", a["nsa_cmp_w2"][0].transpose(1, 0, 2)), ("pe", pe), ("b1", a["nsa_cmp_b1"][0].T)):
        prm[:, slice(*PR[name])] = v.reshape(P, -1)

    def block_pairs(x):
        out = np.zeros((2, 64, SC, 2, 16), x.dtype)
        y = x.reshape(SC, 2, 64, 16)
        for g in range(2):
            out[g, :, :, g] = y[:, g].swapaxes(0, 1)
        return out.reshape(P, SC * 32)
    bmat = np.concatenate([block_pairs(a[n][0]) for n in ("ssm_b_re", "ssm_b_im")], 1)
    cmat = np.concatenate([block_pairs(a[n][0].swapaxes(1, 2)) for n in ("ssm_c_re", "ssm_c_im")], 1)
    pool = a["cache_cmp_kv"].shape[1]
    cmp_pages = a["cache_cmp_kv"][0].reshape(pool, 8, 8, 2, H, 2, 64).transpose(0, 3, 6, 5, 2, 4, 1).reshape(pool, P, -1)
    slc = a["cache_slc_kv"][0]
    slck = slc[:, :, :, 0].transpose(0, 3, 2, 1).reshape(pool, 64, H * PAGE)
    slcv = slc[:, :, :, 1].reshape(pool, PAGE, H * 64)
    win = a["cache_win_kv"][0]
    wink = win[:, :, :, 0].transpose(0, 3, 2, 1).reshape(4, P, H * WIN)
    winv = win[:, :, :, 1].reshape(B, 4, P, H * 64).transpose(2, 0, 1, 3).reshape(P, -1)
    mem = a["cache_mem_kv"]
    memk = mem[:, :, :, :, 0].reshape(2, B, NMEM, 2, 2, 64).transpose(0, 4, 5, 1, 3, 2).reshape(2, P, -1)
    memv = mem[:, :, :, :, 1].reshape(2, B, 2, P, 256).transpose(0, 3, 1, 2, 4).reshape(2, P, -1)
    arrays = dict(x=x, mem=feature_major(a["mem_prompt"][0]), cst1=c1, cst2=c2, slcd=slcd, prm=prm, bmat=bmat, cmat=cmat, w8=w8,
                  wglu=slabs(a["ssm_w_glu"][0]), wfi=wfi, wfo=wfo, w1s=w1s, w1p=w1p,
                  pages=a["page_table"].reshape(1, P).astype(np.int32), cmp=cmp_pages, slck=slck, slcv=slcv, wink=wink,
                  winv=winv, memk=memk, memv=memv, winold=win[:, TS:].reshape(B, WIN - TS, H * 128))

    nc = _bacc.Bacc("TRN2", target_bir_lowering=False, num_devices=1)
    sent, args = {}, []
    for name, v in arrays.items():
        v = np.ascontiguousarray(v)
        sent[f"in_{name}"] = v
        args.append(nc.dram_tensor(f"in_{name}", v.shape, mybir.dt.from_np(v.dtype), kind="ExternalInput").ap())
    for name, shape in _OUTS:
        args.append(nc.dram_tensor(f"out_{name}", shape, F32, kind="ExternalOutput").ap())
    trunk_kernel(nc, *args)
    r = _run(nc, [sent], core_ids=[0]).results[0]
    got = {name: r[f"out_{name}"] for name, _ in _OUTS}
    y = got["y"].reshape(P, KC, T).transpose(2, 1, 0).reshape(T, D)
    stp = got["state_prompt"].reshape(P, 2, SC).transpose(1, 2, 0).reshape(2, 1, 1, GRP, 64)
    sts = got["state_sample"].reshape(P, 2, SC, B).transpose(1, 3, 2, 0).reshape(2, 1, B, GRP, 64)
    kv = got["kv"].reshape(2, 64, 3, H, T).transpose(2, 4, 3, 0, 1)
    kvp = kv[:, :TP].reshape(3, 1, 1, TP, H, 2, 64)
    kvs = kv[:, TP:].reshape(3, 1, B, TS, H, 2, 64)
    win_s = np.concatenate([got["win_old"].reshape(1, B, WIN - TS, H, 2, 64), kvs[2]], 2)
    mkv = got["mem_kv"].reshape(2, P, 2, 2, 2, 2, 64).transpose(0, 2, 1, 3, 5, 4, 6).reshape(2, 1, NMEM, 4, 2, 64)
    return (y[:TP].reshape(1, TP, D), y[TP:].reshape(B, TS, D), stp[0], stp[1], sts[0], sts[1],
            kvp[0], kvp[1], kvp[2], kvs[0], kvs[1], win_s, mkv)
```
